# Optimizing a Trainium2 kernel written in Bass

```python
import jax, jax.numpy as jnp
from jax import lax
import numpy as np

D_MODEL = 2048
BATCH = 1
SEQ = 256
DEPTH = 1

MEM_LEN = 256
D_FF = 5632
FFN_RES = 0.5
D_MIX = D_MODEL
D_CONV_A = D_MIX // 2
D_CONV_B = D_MIX - D_CONV_A
CH_GROUP = 64
N_GROUPS_A = D_CONV_A // CH_GROUP
N_GROUPS_B = D_CONV_B // CH_GROUP
K_SHORT = 3
K_CONF = 31
D_IN_PROJ = 3 * D_CONV_A + 2 * D_CONV_B
N_MEM_HEADS = 4
MEM_HEAD_DIM = D_MODEL // N_MEM_HEADS
RMS_EPS = 1e-6
LN_EPS = 1e-5

kernel_name = "hybrid_shortconv_conformer_macaron_block"

def rmsnorm(x, g):
    xf = x.astype(jnp.float32)
    y = xf * lax.rsqrt(jnp.mean(xf * xf, axis=-1, keepdims=True) + RMS_EPS)
    return (y * g.astype(jnp.float32)).astype(x.dtype)

def layernorm(x, g, b):
    xf = x.astype(jnp.float32)
    mu = jnp.mean(xf, axis=-1, keepdims=True)
    var = jnp.mean(jnp.square(xf - mu), axis=-1, keepdims=True)
    y = (xf - mu) * lax.rsqrt(var + LN_EPS)
    return (y * g.astype(jnp.float32) + b.astype(jnp.float32)).astype(x.dtype)

def causal_depthwise_conv(x, w):
    k, c = w.shape
    return lax.conv_general_dilated(
        x, w[:, None, :].astype(x.dtype), window_strides=(1,), padding=((k - 1, 0),),
        dimension_numbers=("NWC", "WIO", "NWC"), feature_group_count=c)

def swiglu_ffn(u, w_gate_up, w_down):
    gu = jnp.einsum("bsd,df->bsf", u, w_gate_up)
    g, up = jnp.split(gu, 2, axis=-1)
    return jnp.einsum("bsf,fd->bsd", jax.nn.silu(g) * up, w_down)

def parallel_conv_mixer(u, w_in, conv_a_w, conv_b_w, conv_b_bias, ln_b_gain, ln_b_bias, w_out):
    z = jnp.einsum("bsd,de->bse", u, w_in)
    b_gate, c_gate, xa, vb, gb = jnp.split(
        z, [D_CONV_A, 2 * D_CONV_A, 3 * D_CONV_A, 3 * D_CONV_A + D_CONV_B], axis=-1)
    ya = b_gate * causal_depthwise_conv(c_gate * xa, conv_a_w)
    hb = vb * jax.nn.sigmoid(gb)
    hb = causal_depthwise_conv(hb, conv_b_w) + conv_b_bias.astype(hb.dtype)
    yb = jax.nn.silu(layernorm(hb, ln_b_gain, ln_b_bias))
    y = jnp.concatenate([ya, yb], axis=-1)
    return jnp.einsum("bse,ed->bsd", y, w_out)

def memory_cross_attention(u, mem_n, w_q, w_kv, w_o):
    b, s, _ = u.shape
    m = mem_n.shape[1]
    q = jnp.einsum("bsd,de->bse", u, w_q).reshape(b, s, N_MEM_HEADS, MEM_HEAD_DIM)
    kv = jnp.einsum("bmd,de->bme", mem_n, w_kv)
    k, v = jnp.split(kv, 2, axis=-1)
    k = k.reshape(b, m, N_MEM_HEADS, MEM_HEAD_DIM)
    v = v.reshape(b, m, N_MEM_HEADS, MEM_HEAD_DIM)
    scores = jnp.einsum("bshk,bmhk->bhsm", q, k).astype(jnp.float32) * (MEM_HEAD_DIM ** -0.5)
    p = jax.nn.softmax(scores, axis=-1).astype(v.dtype)
    o = jnp.einsum("bhsm,bmhk->bshk", p, v).reshape(b, s, N_MEM_HEADS * MEM_HEAD_DIM)
    return jnp.einsum("bse,ed->bsd", o, w_o)

def setup_inputs(seed: int = 0) -> dict:
    key = jax.random.key(seed)
    ks = jax.random.split(key, 24)
    f32 = jnp.float32

    def nrm(k, shape, fan_in):
        return jax.random.normal(k, shape, f32) * (fan_in ** -0.5)

    def gain(k, shape):
        return 1.0 + 0.02 * jax.random.normal(k, shape, f32)

    L, D = DEPTH, D_MODEL
    return {
        "x": jax.random.normal(ks[0], (BATCH, SEQ, D), f32),
        "mem": jax.random.normal(ks[1], (BATCH, MEM_LEN, D), f32),
        "ffn1_norm": gain(ks[2], (L, D)),
        "ffn1_w_gate_up": nrm(ks[3], (L, D, 2 * D_FF), D),
        "ffn1_w_down": nrm(ks[4], (L, D_FF, D), D_FF),
        "mix_norm": gain(ks[5], (L, D)),
        "w_mix_in": nrm(ks[6], (L, D, D_IN_PROJ), D),
        "conv_a_w": nrm(ks[7], (L, K_SHORT, D_CONV_A), K_SHORT),
        "conv_b_w": nrm(ks[8], (L, K_CONF, D_CONV_B), K_CONF),
        "conv_b_bias": 0.02 * jax.random.normal(ks[9], (L, D_CONV_B), f32),
        "ln_b_gain": gain(ks[10], (L, D_CONV_B)),
        "ln_b_bias": 0.02 * jax.random.normal(ks[11], (L, D_CONV_B), f32),
        "w_mix_out": nrm(ks[12], (L, D_MIX, D), D_MIX),
        "mem_q_norm": gain(ks[13], (L, D)),
        "mem_kv_norm": gain(ks[14], (L, D)),
        "w_mem_q": nrm(ks[15], (L, D, N_MEM_HEADS * MEM_HEAD_DIM), D),
        "w_mem_kv": nrm(ks[16], (L, D, 2 * N_MEM_HEADS * MEM_HEAD_DIM), D),
        "w_mem_o": nrm(ks[17], (L, N_MEM_HEADS * MEM_HEAD_DIM, D), N_MEM_HEADS * MEM_HEAD_DIM),
        "ffn2_norm": gain(ks[18], (L, D)),
        "ffn2_w_gate_up": nrm(ks[19], (L, D, 2 * D_FF), D),
        "ffn2_w_down": nrm(ks[20], (L, D_FF, D), D_FF),
        "final_norm": gain(ks[21], (D,)),
    }

def reference(x, mem, ffn1_norm, ffn1_w_gate_up, ffn1_w_down, mix_norm, w_mix_in, conv_a_w,
              conv_b_w, conv_b_bias, ln_b_gain, ln_b_bias, w_mix_out, mem_q_norm, mem_kv_norm,
              w_mem_q, w_mem_kv, w_mem_o, ffn2_norm, ffn2_w_gate_up, ffn2_w_down, final_norm):
    h = x
    for l in range(DEPTH):
        h = h + FFN_RES * swiglu_ffn(rmsnorm(h, ffn1_norm[l]), ffn1_w_gate_up[l], ffn1_w_down[l])
        h = h + parallel_conv_mixer(rmsnorm(h, mix_norm[l]), w_mix_in[l], conv_a_w[l], conv_b_w[l],
                                    conv_b_bias[l], ln_b_gain[l], ln_b_bias[l], w_mix_out[l])
        h = h + memory_cross_attention(rmsnorm(h, mem_q_norm[l]), rmsnorm(mem, mem_kv_norm[l]),
                                       w_mem_q[l], w_mem_kv[l], w_mem_o[l])
        h = h + FFN_RES * swiglu_ffn(rmsnorm(h, ffn2_norm[l]), ffn2_w_gate_up[l], ffn2_w_down[l])
    return rmsnorm(h, final_norm)


_drawn_inputs = setup_inputs


def setup_inputs(seed=0):
    import zlib

    import numpy as np

    out = dict(_drawn_inputs(seed))
    spreads = {}
    factors = {'ffn1_norm': 5.225,
     'mix_norm': 2.713,
     'conv_b_bias': 3.979,
     'ln_b_gain': 29.059,
     'ln_b_bias': 21.859,
     'mem_q_norm': 8.0,
     'mem_kv_norm': 8.0,
     'ffn2_norm': 23.152,
     'final_norm': 21.228}
    for name, (base, spread) in spreads.items():
        noise = np.random.default_rng([zlib.crc32(name.encode()), seed]).standard_normal(out[name].shape)
        drawn = base * np.exp(spread * noise) if base else spread * noise
        out[name] = __import__('jax').numpy.asarray(drawn.astype(out[name].dtype))
    for name, factor in factors.items():
        out[name] = (out[name] * factor).astype(out[name].dtype)
    return out
```

```python
import concourse.bass as bass
from concourse import mybir
from contextlib import ExitStack

P = 128
TOKENS = 256
HALVES = TOKENS // P
D = 2048
DC = D // P
FF = 5632
FC = FF // P
CA = D // 2
CB = D - CA
KS, KC = 3, 31
HEADS = 4
HD = D // HEADS
HC = HD // P
RMS_EPS, LN_EPS = 1e-6, 1e-5
SEG = 512
COLS = 2 * SEG
RAW, RING = 8, 4
AHEAD = 3

GU = FF // SEG
FFN1 = 0
DOWN1 = FFN1 + GU
MIX_HB = DOWN1 + 2
MIX_CX = MIX_HB + 2
MIX_BG = MIX_CX + 2
MEM_K = MIX_BG + 1
MEM_V = MEM_K + 2
MIX_OUT = MEM_V + 2
MEM_Q = MIX_OUT + 2
MEM_O = MEM_Q + 2
FFN2 = MEM_O + 2
DOWN2 = FFN2 + GU
GROUPS = DOWN2 + 2
NSTEPS = [FC if DOWN1 <= g < DOWN1 + 2 or g >= DOWN2 else DC for g in range(GROUPS)]
BASE = [sum(NSTEPS[:g]) for g in range(GROUPS + 1)]

X_ROUNDS = DC // 4


def rounds_of(g):
    if g >= DOWN2 or MEM_V <= g < MIX_OUT:
        return 0
    if g < DOWN1 or FFN2 <= g or MIX_HB <= g < MIX_BG:
        return 1
    return 2


MEM_ROUNDS = {MIX_CX: (0, 1), MIX_CX + 1: (2, 3)}
ATTN = {MEM_O - 1: 0, MEM_O: 1}
ATTN_ROUNDS = 3


def turned_before(g):
    n = X_ROUNDS + 1
    for at in range(1, g):
        n += rounds_of(at - 1) + len(MEM_ROUNDS.get(at, ())) + (ATTN_ROUNDS if at in ATTN else 0)
    return n


def copied_rounds(g):
    return MIX_HB <= g < MIX_BG


def taken_before(g):
    n = X_ROUNDS
    for at in range(1, g):
        n += (0 if copied_rounds(at - 1) else rounds_of(at - 1)) + len(MEM_ROUNDS.get(at, ()))
        n += ATTN_ROUNDS if at in ATTN else 0
    return n


def highs_before(g):
    return taken_before(g) - (2 if g > MIX_BG + 1 else 0)


def paired(g):
    return g < DOWN1 or MIX_HB <= g < MIX_BG or FFN2 <= g < DOWN2


def gated_before(g):
    return 2 * sum(paired(at) for at in range(g))


PARAMS = [("ffn1_norm", DC), ("mix_norm", DC), ("mem_q_norm", DC), ("mem_kv_norm", DC),
          ("ffn2_norm", DC), ("conv_b_bias", 8), ("ln_b_gain", 8), ("ln_b_bias", 8),
          ("conv_a_w", KS * 8), ("conv_b_w", KC * 8), ("conv_b_bias", 8)]
PCOL = {}
for _name, _n in PARAMS:
    PCOL.setdefault(_name, sum(n for _, n in PARAMS[:len(PCOL)]))
PTILES = 3
assert sum(n for _, n in PARAMS) == PTILES * P

TAPS = 3
CONV_B_OPS = 8 * KC
ST_FFN1, ST_MIX, ST_MEM, ST_Q, ST_FFN2, ST_FINAL = range(6)


def block_program(nc, x, mem, ffn1_norm, ffn1_w_gate_up, ffn1_w_down, mix_norm, w_mix_in, conv_a_w,
                  conv_b_w, conv_b_bias, ln_b_gain, ln_b_bias, w_mix_out, mem_q_norm, mem_kv_norm,
                  w_mem_q, w_mem_kv, w_mem_o, ffn2_norm, ffn2_w_gate_up, ffn2_w_down, final_norm,
                  out):
    f32, f32r = mybir.dt.float32, mybir.dt.float32r
    ALU, ACT, AX = mybir.AluOpType, mybir.ActivationFunctionType, mybir.AxisListType
    params = dict(ffn1_norm=ffn1_norm, mix_norm=mix_norm, mem_q_norm=mem_q_norm,
                  mem_kv_norm=mem_kv_norm, ffn2_norm=ffn2_norm, conv_b_bias=conv_b_bias,
                  ln_b_gain=ln_b_gain, ln_b_bias=ln_b_bias, conv_a_w=conv_a_w, conv_b_w=conv_b_w)

    def weights_of(g):
        if g < DOWN1:
            return ffn1_w_gate_up[0], g * SEG, FF + g * SEG
        if g < MIX_HB:
            w, c = ffn1_w_down[0], (g - DOWN1) * COLS
        elif g < MIX_CX:
            c = 3 * CA + (g - MIX_HB) * SEG
            return w_mix_in[0], c, c + CB
        elif g < MIX_BG:
            c = CA + (g - MIX_CX) * SEG
            return w_mix_in[0], c, c + CA
        elif g < MEM_K:
            w, c = w_mix_in[0], 0
        elif g < MIX_OUT:
            w, c = w_mem_kv[0], (g - MEM_K) * COLS
        elif g < MEM_Q:
            w, c = w_mix_out[0], (g - MIX_OUT) * COLS
        elif g < MEM_O:
            w, c = w_mem_q[0], (g - MEM_Q) * COLS
        elif g < FFN2:
            w, c = w_mem_o[0], (g - MEM_O) * COLS
        elif g < DOWN2:
            return ffn2_w_gate_up[0], (g - FFN2) * SEG, FF + (g - FFN2) * SEG
        else:
            w, c = ffn2_w_down[0], (g - DOWN2) * COLS
        return w, c, c + SEG

    ctx = ExitStack()
    with ctx:
        def sb(name, shape, dt=f32):
            return ctx.enter_context(nc.sbuf_tensor(name, shape, dt))

        def sem(name):
            return ctx.enter_context(nc.semaphore(name))

        h = sb("h", [P, HALVES, D])
        act_hi = sb("act_hi", [P, DC, TOKENS], f32r)
        act_lo = sb("act_lo", [P, DC, TOKENS], f32r)
        raw = sb("raw", [P, RAW, COLS])
        w_hi = sb("w_hi", [P, RING, COLS], f32r)
        w_lo = sb("w_lo", [P, RING, COLS], f32r)
        gated = sb("gated", [P, 4, 256])
        identity = sb("identity", [P, P])
        ones = sb("ones", [P, P])
        pcol = sb("pcol", [P, PTILES * P])
        ssq = sb("ssq", [P, 6, 2, HALVES])
        var = sb("var", [P, 6, HALVES])
        root = sb("root", [P, 6, HALVES])
        newton = sb("newton", [P, 6, HALVES])
        rstd = sb("rstd", [P, 6, HALVES])
        smax = sb("smax", [P, 4])
        nmax = sb("nmax", [P, 4])
        psum_p = sb("psum_p", [P, 4])
        rsum_p = sb("rsum_p", [P, 4])

        with nc.sbuf_tensor("tok", [P, HALVES, COLS], f32) as tok:
            pass
        with nc.sbuf_tensor("p_hi", [P, 4, TOKENS], f32r) as p_hi, \
                nc.sbuf_tensor("p_lo", [P, 4, TOKENS], f32r) as p_lo:
            pass
        tok_place = sb("tok_place", [P, HALVES * COLS])
        param_rows = tok[:, 0, 0:PTILES * P].rearrange("p (t n) -> p t n", t=PTILES)
        final_gain = tok[:, :, :].rearrange("p a n -> p (a n)")
        squares = tok[:, :, :].rearrange("p a (c t) -> p (a c) t", t=TOKENS)

        kb = 256
        with nc.sbuf_tensor("ffn_hi", [P, FC, TOKENS], f32r) as ffn_hi, \
                nc.sbuf_tensor("ffn_lo", [P, FC, TOKENS], f32r) as ffn_lo:
            pass
        with nc.sbuf_tensor("mem_hi", [P, DC, TOKENS], f32r) as mem_hi, \
                nc.sbuf_tensor("mem_lo", [P, DC, TOKENS], f32r) as mem_lo, \
                nc.sbuf_tensor("k_hi", [P, DC, TOKENS], f32r) as k_hi, \
                nc.sbuf_tensor("k_lo", [P, DC, TOKENS], f32r) as k_lo, \
                nc.sbuf_tensor("v_hi0", [P, HALVES, COLS], f32r) as v_hi0, \
                nc.sbuf_tensor("v_lo0", [P, HALVES, COLS], f32r) as v_lo0, \
                nc.sbuf_tensor("v_hi1", [P, HALVES, COLS], f32r) as v_hi1, \
                nc.sbuf_tensor("v_lo1", [P, HALVES, COLS], f32r) as v_lo1:
            v_hi, v_lo = (v_hi0, v_hi1), (v_lo0, v_lo1)
        with nc.sbuf_tensor("uq_hi", [P, DC, TOKENS], f32r) as uq_hi, \
                nc.sbuf_tensor("uq_lo", [P, DC, TOKENS], f32r) as uq_lo, \
                nc.sbuf_tensor("mem_raw", [P, HALVES, D], f32) as mem_raw:
            pass
        with nc.sbuf_tensor("place0", [P, 64 * kb], f32), \
                nc.sbuf_tensor("hb", [P, 8, KC - 1 + TOKENS], f32) as hb, \
                nc.sbuf_tensor("cx", [P, 4, KS - 1 + TOKENS], f32) as cx:
            pass
        with nc.sbuf_tensor("place1", [P, 80 * kb], f32), \
                nc.sbuf_tensor("conv_b", [P, 8, TOKENS], f32) as conv_b, \
                nc.sbuf_tensor("conv_a", [P, 8, TOKENS], f32) as conv_a:
            pass
        sb("large_place", [P, 96 * kb])

        banks = ctx.enter_context(nc.psum_tensor("banks", [P, 2, HALVES, 2, SEG], f32))

        landed = [sem(f"landed{n}") for n in range(RAW // 2)]
        hi_ready = sem("hi_ready")
        lo_ready = sem("lo_ready")
        steps_done = sem("steps_done")
        params_in = sem("params_in")
        x_in = sem("x_in")
        mem_in = sem("mem_in")
        consts_ready = sem("consts_ready")
        const_zero = sem("const_zero")
        pcol_ready = sem("pcol_ready")
        pads_ready = sem("pads_ready")
        gated_ready = sem("gated_ready")
        drained = sem("drained")
        turned = sem("turned")
        high_made = sem("high_made")
        v_high_made = sem("v_high_made")
        taken = sem("taken")
        copied = sem("copied")
        h_ready = sem("h_ready")
        ssq_ready = sem("ssq_ready")
        var_ready = sem("var_ready")
        root_ready = sem("root_ready")
        rstd_ready = sem("rstd_ready")
        dve_chain = sem("dve_chain")
        conv_b_ops = sem("conv_b_ops")
        conv_a_ops = sem("conv_a_ops")
        ya_high = sem("ya_high")
        y_ready = sem("y_ready")
        ln_sum = sem("ln_sum")
        ln_diff = sem("ln_diff")
        ln_square = sem("ln_square")
        ln_var = sem("ln_var")
        ln_root = sem("ln_root")
        ln_normed = sem("ln_normed")
        yb_ready = sem("yb_ready")
        yb_high = sem("yb_high")
        scores_ready = sem("scores_ready")
        nmax_ready = sem("nmax_ready")
        exp_ready = sem("exp_ready")
        p_ready = sem("p_ready")
        final_gain_in = sem("final_gain_in")
        out_ready = sem("out_ready")
        out_stored = sem("out_stored")

        block = ctx.enter_context(nc.Block())

        def round_banks(g, r):
            return banks[:, (g + 1) % 2, r % 2, :, :].rearrange("p s (c t) -> p (s c) t", t=TOKENS)

        @block.sync
        def _(sp):
            def load_steps(g, k, base, shift=0, wait=True):
                n = BASE[g] + k
                slot = n % RAW
                if wait:
                    sp.wait_ge(lo_ready, base + (k + 2 - RAW))
                w, c0, c1 = weights_of(g)
                c0, c1 = c0 + shift, c1 + shift
                for s, c in enumerate((c0, c1)):
                    rows = w[k * P:(k + 2) * P, bass.ds(c, SEG)].rearrange("(a p) n -> p a n", p=P)
                    sp.dma_start(raw[:, slot:slot + 2, s * SEG:(s + 1) * SEG], rows) \
                      .then_inc(landed[slot // 2], 16)

            def load_wide(g, k):
                n = BASE[g] + k
                slot = n % RAW
                sp.wait_ge(lo_ready, n + 2 - RAW)
                w, c0, _ = weights_of(g)
                for a in range(2):
                    sp.dma_start(raw[:, slot + a, :], w[(k + a) * P:(k + a + 1) * P, c0:c0 + COLS]) \
                      .then_inc(landed[slot // 2], 16)

            row = 0
            for name, n in PARAMS:
                v = params[name][0]
                v = v.rearrange("k (c p) -> (k c) p", p=P) if len(v.shape) == 2 else \
                    v.rearrange("(c p) -> c p", p=P)
                done = 0
                while done < n:
                    m = min(n - done, P - row % P)
                    sp.dma_start(param_rows[row % P:row % P + m, row // P, :], v[done:done + m, :]) \
                      .then_inc(params_in, 16)
                    done += m
                    row += m
            for t in range(HALVES):
                sp.dma_start(h[:, t, :], x[0, t * P:(t + 1) * P, :]).then_inc(x_in, 16)

            def gate_up(first):
                for k in range(0, DC, 2):
                    load_steps(first, k, BASE[first], wait=BASE[first] + k >= RAW)
                with sp.Fori(0, (GU - 1) // 2) as i:
                    for j in range(2):
                        for k in range(0, DC, 2):
                            load_steps(first + 1 + j, k, BASE[first + 1 + j] + i * (2 * DC),
                                       shift=i * (2 * SEG))

            gate_up(FFN1)
            for g in range(DOWN1, FFN2):
                for k in range(0, NSTEPS[g], 2):
                    if g == MIX_HB and k == 8:
                        sp.wait_ge(steps_done, BASE[MIX_HB])
                        for t in range(HALVES):
                            sp.dma_start(mem_raw[:, t, :], mem[0, t * P:(t + 1) * P, :]) \
                              .then_inc(mem_in, 16)
                    if MIX_HB <= g < MIX_BG:
                        load_steps(g, k, BASE[g])
                    else:
                        load_wide(g, k)
            gate_up(FFN2)
            for g in range(DOWN2, GROUPS):
                for k in range(0, NSTEPS[g], 2):
                    load_wide(g, k)
                    if g == DOWN2 and k == 16:
                        sp.wait_ge(turned, turned_before(DOWN2 + 1))
                        sp.dma_start(final_gain, final_norm.rearrange("(a n) -> a n", a=1)
                                     .partition_broadcast(P)).then_inc(final_gain_in, 16)
            for n in range(2 * HALVES):
                t, c = n // 2, n % 2 * COLS
                sp.wait_ge(out_ready, n + 1)
                sp.dma_start(out[0, t * P:(t + 1) * P, c:c + COLS], h[:, t, c:c + COLS]) \
                  .then_inc(out_stored, 16)
            sp.wait_ge(out_stored, 16 * 2 * HALVES)

        @block.gpsimd
        def _(pool):
            nc.gpsimd.memset(ones[:, :], 1.0).then_inc(consts_ready, 1)
            nc.gpsimd.memset(identity[:, :], 0.0).then_inc(const_zero, 1)
            pool.wait_ge(const_zero, 1)
            nc.gpsimd.affine_select(out=identity[:, :], in_=identity[:, :],
                                    compare_op=ALU.not_equal, fill=1.0, base=0,
                                    pattern=[[-1, P]], channel_multiplier=1).then_inc(consts_ready, 1)
            pool.wait_ge(steps_done, BASE[MIX_HB])
            nc.gpsimd.memset(hb[:, :, 0:KC - 1], 0.0).then_inc(pads_ready, 1)
            nc.gpsimd.memset(cx[:, :, 0:KS - 1], 0.0).then_inc(pads_ready, 1)

        @block.scalar
        def _(act):
            def highs(g, k0, k1, off=0):
                for k in range(k0, k1):
                    n = BASE[g] + k
                    act.wait_ge(landed[n % RAW // 2], (n // RAW + 1) * 32 + off * (32 // RAW))
                    if n >= RING:
                        act.wait_ge(steps_done, n + 1 - RING + off)
                    nc.scalar.activation(w_hi[:, n % RING, :], raw[:, n % RAW, :], ACT.Copy) \
                        .then_inc(hi_ready, 1)

            def high_round(g, r, dst, chunk, gain, number):
                act.wait_ge(turned, number)
                src = round_banks(g, r)
                if gain is None:
                    last = nc.scalar.activation(dst[:, bass.ds(chunk, 4), :], src, ACT.Copy)
                else:
                    for c in range(4):
                        col = PCOL[gain] + chunk + c
                        last = nc.scalar.activation(dst[:, chunk + c, :], src[:, c, :], ACT.Copy,
                                                    scale=pcol[:, col:col + 1])
                last.then_inc(high_made, 1)

            def gate(g, func, seg, stat, off=0):
                act.wait_ge(steps_done, BASE[g + 1] + off)
                act.wait_ge(rstd_ready, stat + 1)
                for t in range(HALVES):
                    nc.scalar.activation(gated[:, 2 * t:2 * t + 2, :].rearrange("p a n -> p (a n)"),
                                         banks[:, g % 2, t, seg, :], func,
                                         scale=rstd[:, stat, t:t + 1]).then_inc(gated_ready, 1)

            def drain_scaled(g, stat):
                act.wait_ge(steps_done, BASE[g + 1])
                act.wait_ge(rstd_ready, stat + 1)
                for t in range(HALVES):
                    for s in range(2):
                        last = nc.scalar.activation(tok[:, t, s * SEG:(s + 1) * SEG],
                                                    banks[:, g % 2, t, s, :], ACT.Copy,
                                                    scale=rstd[:, stat, t:t + 1])
                last.then_inc(drained, 1)

            def squares_of(src, stat, part, cols):
                for t in range(HALVES):
                    before = 4 * stat + 2 * part + t
                    if before:
                        act.wait_ge(ssq_ready, before)
                    nc.scalar.activation(tok_junk(cols), src[:, t, part * cols:(part + 1) * cols],
                                         ACT.Square, accum_out=ssq[:, stat, part, t:t + 1]) \
                        .then_inc(ssq_ready, 1)

            def tok_junk(cols):
                return gated[:, :, :].rearrange("p a n -> p (a n)")[:, 0:cols]

            def square_root(stat):
                act.wait_ge(var_ready, stat + 1)
                nc.scalar.activation(root[:, stat, :], var[:, stat, :], ACT.Sqrt) \
                    .then_inc(root_ready, 1)

            def residual_squares(g, part, stat):
                act.wait_ge(h_ready, 2 * stat_order.index(stat) + part + 1)
                squares_of(h, stat, part, COLS)

            stat_order = [ST_MIX, ST_Q, ST_FFN2, ST_FINAL]

            act.wait_ge(turned, 1)
            nc.scalar.activation(pcol[:, :], banks[:, 1, 0, 0, 0:PTILES * P], ACT.Copy) \
                .then_inc(pcol_ready, 1)
            act.wait_ge(pcol_ready, 1)
            for r in range(X_ROUNDS):
                high_round(FFN1, r, act_hi, 4 * r, "ffn1_norm", 2 + r)
            highs(FFN1, 0, AHEAD + 1)
            for part in range(2):
                squares_of(h, ST_FFN1, part, COLS)
            highs(FFN1, AHEAD + 1, 6)
            square_root(ST_FFN1)
            highs(FFN1, 6, DC)

            def gate_up(first, stat):
                with act.Fori(0, (GU - 1) // 2) as i:
                    for j in range(2):
                        g = first + 1 + j
                        highs(g, 0, AHEAD, i * (2 * DC))
                        gate(g - 1, ACT.Silu, 0, stat, i * (2 * DC))
                        highs(g, AHEAD, 7, i * (2 * DC))
                        high_round(g, 0, ffn_hi, i * 8 + 4 * j, None, turned_before(g) + 1 + i * 2)
                        highs(g, 7, DC, i * (2 * DC))
                g = first + GU
                highs(g, 0, AHEAD)
                gate(g - 1, ACT.Silu, 0, stat)
                highs(g, AHEAD, 7)
                high_round(g, 0, ffn_hi, FC - 4, None, turned_before(g) + 1)
                long_highs(g, 7)

            def long_highs(g, k0):
                k1 = NSTEPS[g] - (NSTEPS[g] - k0) % RAW
                with act.Fori(0, (k1 - k0) // RAW) as i:
                    highs(g, k0, k0 + RAW, i * RAW)
                highs(g, k1, NSTEPS[g])

            gate_up(FFN1, ST_FFN1)

            def residual_group(g, part, stat, dst, gain):
                highs(g, 0, AHEAD)
                residual_squares(g - 1, part, stat)
                highs(g, AHEAD, 5)
                if part == 1:
                    square_root(stat)
                highs(g, 5, 7)
                for r in range(2):
                    high_round(g, r, dst, 8 * part + 4 * r, gain, turned_before(g) + 1 + r)

            residual_group(DOWN1 + 1, 0, ST_MIX, act_hi, "mix_norm")
            long_highs(DOWN1 + 1, 7)
            residual_group(MIX_HB, 1, ST_MIX, act_hi, "mix_norm")
            highs(MIX_HB, 7, DC)

            def copy_round(g, dst, pad, number):
                act.wait_ge(turned, number)
                nc.scalar.activation(dst[:, :, pad:pad + TOKENS], round_banks(g, 0), ACT.Copy) \
                    .then_inc(copied, 1)

            for j in range(2):
                g = MIX_HB + 1 + j
                highs(g, 0, AHEAD)
                gate(g - 1, ACT.Sigmoid, 1, ST_MIX)
                highs(g, AHEAD, 7)
                if j == 0:
                    act.wait_ge(pads_ready, 2)
                copy_round(g, hb[:, 4 * j:4 * j + 4, :], KC - 1, turned_before(g) + 1)
                highs(g, 7, 8)
                if j == 0:
                    act.wait_ge(mem_in, 32)
                    for part in range(2):
                        squares_of(mem_raw, ST_MEM, part, COLS)
                    highs(g, 8, 10)
                    square_root(ST_MEM)
                else:
                    for m, r in enumerate(MEM_ROUNDS[g]):
                        high_round(g, m + 1, mem_hi, 4 * r, "mem_kv_norm", turned_before(g) + 2 + m)
                highs(g, 10 if j == 0 else 8, DC)
            for j in range(2):
                g = MIX_CX + 1 + j
                highs(g, 0, AHEAD)
                gate(g - 1, ACT.Copy, 0, ST_MIX)
                highs(g, AHEAD, 7)
                if j == 1:
                    act.wait_ge(conv_a_ops, 4 * KS)
                copy_round(g, cx[:, :, :], KS - 1, turned_before(g) + 1)
                highs(g, 7, 8)
                if g in MEM_ROUNDS:
                    for m, r in enumerate(MEM_ROUNDS[g]):
                        high_round(g, m + 1, mem_hi, 4 * r, "mem_kv_norm", turned_before(g) + 2 + m)
                highs(g, 8, DC)
            highs(MEM_K, 0, AHEAD)
            drain_scaled(MIX_BG, ST_MIX)
            highs(MEM_K, AHEAD, 8)
            act.wait_ge(taken, taken_before(MEM_K) + 2)
            nc.scalar.activation(act_hi[:, 0:8, :], conv_a[:, :, :], ACT.Copy).then_inc(ya_high, 1)
            highs(MEM_K, 8, DC)
            for j in range(2):
                g = MEM_K + 1 + j
                highs(g, 0, AHEAD)
                drain_scaled(g - 1, ST_MEM)
                highs(g, AHEAD, 7)
                for r in range(2):
                    high_round(g, r, k_hi, 8 * j + 4 * r, None, turned_before(g) + 1 + r)
                highs(g, 7, DC)

            def drain_v(j):
                act.wait_ge(steps_done, BASE[MEM_V + j + 1])
                if j == 0:
                    act.wait_ge(conv_b_ops, CONV_B_OPS)
                else:
                    act.wait_ge(y_ready, 2)
                for t in range(HALVES):
                    for s in range(2):
                        last = nc.scalar.activation(v_hi[j][:, t, s * SEG:(s + 1) * SEG],
                                                    banks[:, (MEM_V + j) % 2, t, s, :], ACT.Copy,
                                                    scale=rstd[:, ST_MEM, t:t + 1])
                last.then_inc(v_high_made, 1)

            highs(MEM_V + 1, 0, AHEAD)
            drain_v(0)
            highs(MEM_V + 1, AHEAD, 6)
            act.wait_ge(ln_diff, 1)
            nc.scalar.activation(squares, conv_b[:, :, :], ACT.Square).then_inc(ln_square, 1)
            highs(MEM_V + 1, 6, 9)
            act.wait_ge(ln_var, 1)
            nc.scalar.activation(gated[:, 1, :], gated[:, 0, :], ACT.Sqrt).then_inc(ln_root, 1)
            highs(MEM_V + 1, 9, 12)
            act.wait_ge(ln_normed, 1)
            for c in range(8):
                g1, b1 = PCOL["ln_b_gain"] + c, PCOL["ln_b_bias"] + c
                last = nc.scalar.activation(conv_b[:, c, :], conv_b[:, c, :], ACT.Silu,
                                            scale=pcol[:, g1:g1 + 1], bias=pcol[:, b1:b1 + 1])
            last.then_inc(yb_ready, 1)
            act.wait_ge(yb_ready, 1)
            nc.scalar.activation(act_hi[:, 8:16, :], conv_b[:, :, :], ACT.Copy).then_inc(yb_high, 1)
            highs(MEM_V + 1, 12, DC)
            highs(MIX_OUT, 0, AHEAD)
            drain_v(1)
            highs(MIX_OUT, AHEAD, DC)
            residual_group(MIX_OUT + 1, 0, ST_Q, uq_hi, "mem_q_norm")
            highs(MIX_OUT + 1, 7, DC)
            residual_group(MEM_Q, 1, ST_Q, uq_hi, "mem_q_norm")
            highs(MEM_Q, 7, DC)

            for g, at in ((MEM_O - 1, (6, 9, 12, 15)), (MEM_O, (5, 6, 8, 9))):
                pair = ATTN[g]
                number = turned_before(g)
                highs(g, 0, AHEAD)
                drain_scaled(g - 1, ST_Q)
                highs(g, AHEAD, at[0])
                for r in range(2):
                    high_round(g, r, act_hi, 8 * pair + 4 * r, None, number + 1 + r)
                highs(g, at[0], at[1])
                act.wait_ge(nmax_ready, pair + 1)
                for n in range(4):
                    nc.scalar.activation(gated[:, n, :], round_banks(g, 0)[:, n, :], ACT.Exp,
                                         bias=nmax[:, n:n + 1], scale=float(HD) ** -0.5,
                                         accum_out=psum_p[:, n:n + 1]).then_inc(exp_ready, 1)
                highs(g, at[1], at[2])
                high_round(g, 1, p_hi, 0, None, number + 3)
                highs(g, at[2], at[3])
                for r in range(2):
                    high_round(g, r, k_hi, 8 * pair + 4 * r, None, number + 4 + r)
                highs(g, at[3], DC)
            residual_group(MEM_O + 1, 0, ST_FFN2, act_hi, "ffn2_norm")
            highs(MEM_O + 1, 7, DC)
            residual_group(FFN2, 1, ST_FFN2, act_hi, "ffn2_norm")
            highs(FFN2, 7, DC)
            gate_up(FFN2, ST_FFN2)
            highs(DOWN2 + 1, 0, AHEAD)
            residual_squares(DOWN2, 0, ST_FINAL)
            long_highs(DOWN2 + 1, AHEAD)
            residual_squares(DOWN2 + 1, 1, ST_FINAL)
            square_root(ST_FINAL)

        @block.vector
        def _(dve):
            chain = [0]

            def link(instruction):
                chain[0] += 1
                instruction.then_inc(dve_chain, 1)
                dve.wait_ge(dve_chain, chain[0])

            def lows(g, k0, k1, off=0):
                for k in range(k0, k1):
                    n = BASE[g] + k
                    dve.wait_ge(hi_ready, n + 1 + off)
                    nc.vector.tensor_tensor(w_lo[:, n % RING, :], raw[:, n % RAW, :],
                                            w_hi[:, n % RING, :].bitcast(f32), ALU.subtract) \
                        .then_inc(lo_ready, 1)

            def long_lows(g, k0):
                k1 = NSTEPS[g] - (NSTEPS[g] - k0) % RAW
                with dve.Fori(0, (k1 - k0) // RAW) as i:
                    lows(g, k0, k0 + RAW, i * RAW)
                lows(g, k1, NSTEPS[g])

            def low_round(g, r, hi, lo, chunk, gain, number):
                dve.wait_ge(high_made, number)
                src = round_banks(g, r)
                if gain is None:
                    for s in range(2):
                        c = bass.ds(chunk + 2 * s, 2)
                        last = nc.vector.tensor_tensor(lo[:, c, :], src[:, 2 * s:2 * s + 2, :],
                                                       hi[:, c, :].bitcast(f32), ALU.subtract)
                else:
                    for c in range(4):
                        col = PCOL[gain] + chunk + c
                        last = nc.vector.scalar_tensor_tensor(
                            out=lo[:, chunk + c, :], in0=src[:, c, :], scalar=pcol[:, col:col + 1],
                            in1=hi[:, chunk + c, :].bitcast(f32), op0=ALU.mult, op1=ALU.subtract)
                last.then_inc(taken, 1)

            def drain_gated(g, seg, stat, number):
                for t in range(HALVES):
                    dve.wait_ge(gated_ready, number + t + 1)
                    last = nc.vector.scalar_tensor_tensor(
                        out=tok[:, t, 0:SEG], in0=banks[:, g % 2, t, seg, :],
                        scalar=rstd[:, stat, t:t + 1],
                        in1=gated[:, 2 * t:2 * t + 2, :].rearrange("p a n -> p (a n)"),
                        op0=ALU.mult, op1=ALU.mult)
                last.then_inc(drained, 1)

            def add_residual(g, part, factor):
                dve.wait_ge(steps_done, BASE[g + 1])
                for t in range(HALVES):
                    for s in range(2):
                        cols = h[:, t, part * COLS + s * SEG:part * COLS + (s + 1) * SEG]
                        last = nc.vector.scalar_tensor_tensor(
                            out=cols, in0=banks[:, g % 2, t, s, :], scalar=factor, in1=cols,
                            op0=ALU.mult, op1=ALU.add)
                last.then_inc(h_ready, 1)

            def norm_factor(stat, number):
                dve.wait_ge(ssq_ready, 4 * (number + 1))
                link(nc.vector.tensor_tensor(var[:, stat, :], ssq[:, stat, 0, :], ssq[:, stat, 1, :],
                                             ALU.add))
                nc.vector.tensor_scalar(var[:, stat, :], var[:, stat, :], 1.0 / D, RMS_EPS,
                                        ALU.mult, ALU.add).then_inc(var_ready, 1)
                dve.wait_ge(root_ready, number + 1)
                rsqrt(rstd[:, stat, :], var[:, stat, :], root[:, stat, :], newton[:, stat, :],
                      rstd_ready)

            def rsqrt(out_, a, sqrt_a, tmp, done):
                link(nc.vector.reciprocal(out_, sqrt_a))
                link(nc.vector.tensor_tensor(tmp, out_, out_, ALU.mult))
                link(nc.vector.tensor_tensor(tmp, tmp, a, ALU.mult))
                link(nc.vector.tensor_scalar(tmp, tmp, -0.5, 1.5, ALU.mult, ALU.add))
                nc.vector.tensor_tensor(out_, out_, tmp, ALU.mult).then_inc(done, 1)

            def conv_b_taps(first, count):
                for n in range(first, min(first + count, CONV_B_OPS)):
                    c, tap = n // (4 * KC) * 4 + n % 4, n % (4 * KC) // 4
                    w = PCOL["conv_b_w"] + tap * 8 + c
                    src = hb[:, c, tap:tap + TOKENS]
                    if tap == 0:
                        b = PCOL["conv_b_bias"] + c
                        ins = nc.vector.tensor_scalar(conv_b[:, c, :], src, pcol[:, w:w + 1],
                                                      pcol[:, b:b + 1], ALU.mult, ALU.add)
                    else:
                        dve.wait_ge(conv_b_ops, n - 3)
                        ins = nc.vector.scalar_tensor_tensor(
                            out=conv_b[:, c, :], in0=src, scalar=pcol[:, w:w + 1],
                            in1=conv_b[:, c, :], op0=ALU.mult, op1=ALU.add)
                    ins.then_inc(conv_b_ops, 1)

            def conv_a_tap(part, tap):
                for c4 in range(4):
                    c = 4 * part + c4
                    w = PCOL["conv_a_w"] + tap * 8 + c
                    src = cx[:, c4, tap:tap + TOKENS]
                    if tap == 0:
                        ins = nc.vector.tensor_scalar(conv_a[:, c, :], src, pcol[:, w:w + 1], None,
                                                      ALU.mult)
                    else:
                        dve.wait_ge(conv_a_ops, part * 4 * KS + 4 * tap + c4 - 3)
                        ins = nc.vector.scalar_tensor_tensor(
                            out=conv_a[:, c, :], in0=src, scalar=pcol[:, w:w + 1],
                            in1=conv_a[:, c, :], op0=ALU.mult, op1=ALU.add)
                    ins.then_inc(conv_a_ops, 1)

            dve.wait_ge(x_in, 16 * HALVES)
            dve.wait_ge(pcol_ready, 1)
            for r in range(X_ROUNDS):
                low_round(FFN1, r, act_hi, act_lo, 4 * r, "ffn1_norm", r + 1)
            lows(FFN1, 0, 6)
            norm_factor(ST_FFN1, 0)
            lows(FFN1, 6, DC)

            def gate_up(first, stat, order):
                dve.wait_ge(rstd_ready, order + 1)
                with dve.Fori(0, (GU - 1) // 2) as i:
                    for j in range(2):
                        g = first + 1 + j
                        lows(g, 0, AHEAD, i * (2 * DC))
                        drain_gated(g - 1, 1, stat, gated_before(g - 1) + i * 4)
                        lows(g, AHEAD, 7, i * (2 * DC))
                        low_round(g, 0, ffn_hi, ffn_lo, i * 8 + 4 * j, None,
                                  highs_before(g) + 1 + i * 2)
                        lows(g, 7, DC, i * (2 * DC))
                g = first + GU
                lows(g, 0, AHEAD)
                drain_gated(g - 1, 1, stat, gated_before(g - 1))
                lows(g, AHEAD, 7)
                low_round(g, 0, ffn_hi, ffn_lo, FC - 4, None, highs_before(g) + 1)
                long_lows(g, 7)

            gate_up(FFN1, ST_FFN1, 0)

            def residual_group(g, part, factor, stat, order, hi, lo, gain):
                lows(g, 0, AHEAD)
                add_residual(g - 1, part, factor)
                lows(g, AHEAD, 5)
                if part == 1:
                    norm_factor(stat, order)
                lows(g, 5, 7)
                for r in range(2):
                    low_round(g, r, hi, lo, 8 * part + 4 * r, gain,
                              highs_before(g) + 1 + r)

            residual_group(DOWN1 + 1, 0, 0.5, ST_MIX, 1, act_hi, act_lo, "mix_norm")
            long_lows(DOWN1 + 1, 7)
            residual_group(MIX_HB, 1, 0.5, ST_MIX, 1, act_hi, act_lo, "mix_norm")
            lows(MIX_HB, 7, DC)

            g = MIX_HB + 1
            lows(g, 0, AHEAD)
            drain_gated(g - 1, 0, ST_MIX, gated_before(g - 1))
            lows(g, AHEAD, 10)
            norm_factor(ST_MEM, 2)
            dve.wait_ge(copied, 1)
            op = 0
            for k in range(10, DC):
                lows(g, k, k + 1)
                conv_b_taps(op, TAPS)
                op += TAPS
            for g in range(MIX_CX, MEM_V + 1):
                for k in range(AHEAD):
                    lows(g, k, k + 1)
                    conv_b_taps(op, TAPS)
                    op += TAPS
                if g <= MIX_BG:
                    drain_gated(g - 1, 0 if g == MIX_CX else 1, ST_MIX, gated_before(g - 1))
                for k in range(AHEAD, 8):
                    lows(g, k, k + 1)
                    if k < 7:
                        conv_b_taps(op, TAPS)
                        op += TAPS
                if g == MIX_CX:
                    dve.wait_ge(copied, 2)
                if g in MEM_ROUNDS:
                    for m, r in enumerate(MEM_ROUNDS[g]):
                        low_round(g, m + 1, mem_hi, mem_lo, 4 * r, "mem_kv_norm",
                                  highs_before(g) + 1 + m)
                if g == MEM_K:
                    dve.wait_ge(conv_a_ops, 2 * 4 * KS)
                    for r in range(2):
                        dve.wait_ge(turned, turned_before(g) + 1 + r)
                        chunks = conv_a[:, 4 * r:4 * r + 4, :]
                        for s in range(2):
                            part = chunks[:, 2 * s:2 * s + 2, :]
                            last = nc.vector.tensor_tensor(part, round_banks(g, r)[:, 2 * s:2 * s + 2, :],
                                                           part, ALU.mult)
                        last.then_inc(taken, 1)
                if g > MEM_K:
                    for r in range(2):
                        low_round(g, r, k_hi, k_lo, 8 * (g - MEM_K - 1) + 4 * r, None,
                                  highs_before(g) + 1 + r)
                for k in range(8, DC):
                    lows(g, k, k + 1)
                    if g in (MIX_CX + 1, MIX_BG) and k < 8 + KS:
                        if k == 8:
                            dve.wait_ge(copied, 3 + g - MIX_CX - 1)
                        conv_a_tap(g - MIX_CX - 1, k - 8)
                    else:
                        conv_b_taps(op, TAPS)
                        op += TAPS
                    if g == MEM_K and k == 10:
                        dve.wait_ge(ya_high, 1)
                        nc.vector.tensor_tensor(act_lo[:, 0:8, :], conv_a[:, :, :],
                                                act_hi[:, 0:8, :].bitcast(f32), ALU.subtract) \
                            .then_inc(y_ready, 1)
            assert op >= CONV_B_OPS

            def drain_v(j):
                g = MEM_V + j
                dve.wait_ge(v_high_made, j + 1)
                for t in range(HALVES):
                    for s in range(2):
                        cols = slice(s * SEG, (s + 1) * SEG)
                        last = nc.vector.scalar_tensor_tensor(
                            out=v_lo[j][:, t, cols], in0=banks[:, g % 2, t, s, :],
                            scalar=rstd[:, ST_MEM, t:t + 1], in1=v_hi[j][:, t, cols].bitcast(f32),
                            op0=ALU.mult, op1=ALU.subtract)
                last.then_inc(drained, 1)

            g = MEM_V + 1
            sums = round_banks(g, 0)[:, 0, :]
            squared = round_banks(g, 1)[:, 0, :]
            lows(g, 0, AHEAD)
            drain_v(0)
            lows(g, AHEAD, 5)
            dve.wait_ge(ln_sum, 1)
            mean = gated[:, 2, :]
            link(nc.vector.tensor_scalar(mean, sums, 1.0 / CB, None, ALU.mult))
            nc.vector.tensor_tensor(conv_b[:, :, :], conv_b[:, :, :],
                                    mean.unsqueeze(1).to_broadcast([P, 8, TOKENS]), ALU.subtract) \
                .then_inc(ln_diff, 1)
            lows(g, 5, 8)
            dve.wait_ge(ln_sum, 2)
            nc.vector.tensor_scalar(gated[:, 0, :], squared, 1.0 / CB, LN_EPS, ALU.mult, ALU.add) \
                .then_inc(ln_var, 1)
            lows(g, 8, 10)
            dve.wait_ge(ln_root, 1)
            rsqrt(gated[:, 2, :], gated[:, 0, :], gated[:, 1, :], gated[:, 3, :], ln_root)
            dve.wait_ge(ln_root, 2)
            nc.vector.tensor_tensor(conv_b[:, :, :], conv_b[:, :, :],
                                    gated[:, 2, :].unsqueeze(1).to_broadcast([P, 8, TOKENS]),
                                    ALU.mult).then_inc(ln_normed, 1)
            lows(g, 10, 14)
            dve.wait_ge(yb_high, 1)
            nc.vector.tensor_tensor(act_lo[:, 8:16, :], conv_b[:, :, :],
                                    act_hi[:, 8:16, :].bitcast(f32), ALU.subtract) \
                .then_inc(y_ready, 1)
            lows(g, 14, DC)
            lows(MIX_OUT, 0, AHEAD)
            drain_v(1)
            lows(MIX_OUT, AHEAD, DC)
            residual_group(MIX_OUT + 1, 0, 1.0, ST_Q, 3, uq_hi, uq_lo, "mem_q_norm")
            lows(MIX_OUT + 1, 7, DC)
            residual_group(MEM_Q, 1, 1.0, ST_Q, 3, uq_hi, uq_lo, "mem_q_norm")
            lows(MEM_Q, 7, DC)

            for g, at in ((MEM_O - 1, (6, 9, 12, 15)), (MEM_O, (5, 6, 8, 9))):
                pair = ATTN[g]
                number = highs_before(g)
                lows(g, 0, at[0])
                for r in range(2):
                    low_round(g, r, act_hi, act_lo, 8 * pair + 4 * r, None, number + 1 + r)
                lows(g, at[0], at[1])
                dve.wait_ge(scores_ready, pair + 1)
                scores = round_banks(g, 0)
                for s in range(2):
                    last = nc.vector.reduce_max(smax[:, 2 * s:2 * s + 2], scores[:, 2 * s:2 * s + 2, :],
                                                AX.X)
                link(last)
                nc.vector.tensor_scalar(nmax[:, :], smax[:, :], -float(HD) ** -0.5, None, ALU.mult) \
                    .then_inc(nmax_ready, 1)
                dve.wait_ge(exp_ready, 4 * (pair + 1))
                link(nc.vector.reciprocal(rsum_p[:, :], psum_p[:, :]))
                for n in range(4):
                    last = nc.vector.tensor_scalar(gated[:, n, :], gated[:, n, :],
                                                   rsum_p[:, n:n + 1], None, ALU.mult)
                last.then_inc(p_ready, 1)
                lows(g, at[1], at[2])
                low_round(g, 1, p_hi, p_lo, 0, None, number + 3)
                lows(g, at[2], at[3])
                for r in range(2):
                    low_round(g, r, k_hi, k_lo, 8 * pair + 4 * r, None, number + 4 + r)
                lows(g, at[3], DC)
            residual_group(MEM_O + 1, 0, 1.0, ST_FFN2, 4, act_hi, act_lo, "ffn2_norm")
            lows(MEM_O + 1, 7, DC)
            residual_group(FFN2, 1, 1.0, ST_FFN2, 4, act_hi, act_lo, "ffn2_norm")
            lows(FFN2, 7, DC)
            gate_up(FFN2, ST_FFN2, 4)
            lows(DOWN2 + 1, 0, AHEAD)
            add_residual(DOWN2, 0, 0.5)
            long_lows(DOWN2 + 1, AHEAD)
            add_residual(DOWN2 + 1, 1, 0.5)
            norm_factor(ST_FINAL, 5)
            dve.wait_ge(final_gain_in, 16)
            dve.wait_ge(rstd_ready, 6)
            for n in range(2 * HALVES):
                t, c = n // 2, n % 2 * COLS
                nc.vector.scalar_tensor_tensor(
                    out=h[:, t, c:c + COLS], in0=h[:, t, c:c + COLS], scalar=rstd[:, ST_FINAL, t:t + 1],
                    in1=final_gain[:, c:c + COLS], op0=ALU.mult, op1=ALU.mult).then_inc(out_ready, 1)

        @block.tensor
        def _(pe):
            def steps(g, k0, k1, hi, lo, off=0):
                for k in range(k0, k1):
                    n = BASE[g] + k
                    pe.wait_ge(lo_ready, n + 1 + off)
                    first, end = k == 0, k == NSTEPS[g] - 1
                    for t in range(HALVES):
                        tokens = slice(t * P, (t + 1) * P)
                        for a, w in ((hi, w_hi), (hi, w_lo), (lo, w_hi)):
                            for s in range(2):
                                last = nc.tensor.matmul(
                                    banks[:, g % 2, t, s, :], a[:, k, tokens],
                                    w[:, n % RING, s * SEG:(s + 1) * SEG],
                                    start=first and w is w_hi and a is hi,
                                    stop=end and a is lo)
                    last.then_inc(steps_done, 1)

            def turn_round(g, r, source):
                dst = round_banks(g, r)
                for c in range(4):
                    for t in range(HALVES):
                        last = nc.tensor.transpose(dst[:, c, t * P:(t + 1) * P], source(c, t),
                                                   identity[:, :])
                last.then_inc(turned, 1)

            def of_tok(r):
                return lambda c, t: tok[:, t, (4 * r + c) * P:(4 * r + c + 1) * P]

            def of_rows(src, part):
                return lambda c, t: src[:, t, (4 * part + c) * P:(4 * part + c + 1) * P]

            def turn_group(g, off=0):
                pe.wait_ge(drained, drains_before(g - 1) + 1 + off)
                for r in range(rounds_of(g - 1)):
                    turn_round(g, r, of_tok(r))

            def drains_before(g):
                return sum(1 for at in range(g) if not residual(at))

            def residual(g):
                return DOWN1 <= g < MIX_HB or MIX_OUT <= g < MEM_Q or MEM_O <= g < FFN2 or g >= DOWN2

            def turn_residual(g, number):
                part = (number + 1) % 2
                pe.wait_ge(h_ready, number)
                for r in range(2):
                    turn_round(g, r, of_rows(h, 2 * part + r))

            pe.wait_ge(consts_ready, 2)
            pe.wait_ge(params_in, 16 * PARAM_LOADS)
            for n in range(PTILES):
                last = nc.tensor.transpose(banks[:, 1, 0, 0, n * P:(n + 1) * P], param_rows[:, n, :],
                                           identity[:, :])
            last.then_inc(turned, 1)
            pe.wait_ge(x_in, 16 * HALVES)
            pe.wait_ge(pcol_ready, 1)
            for r in range(X_ROUNDS):
                if r >= 2:
                    pe.wait_ge(taken, r - 1)
                turn_round(FFN1, r, of_rows(h, r))
            pe.wait_ge(taken, X_ROUNDS)
            steps(FFN1, 0, DC, act_hi, act_lo)

            def gate_up(first, hi, lo):
                with pe.Fori(0, (GU - 1) // 2) as i:
                    for j in range(2):
                        g = first + 1 + j
                        pe.wait_ge(taken, taken_before(g) + i * 2)
                        steps(g, 0, 4, hi, lo, i * (2 * DC))
                        turn_group(g, i * 2)
                        steps(g, 4, DC, hi, lo, i * (2 * DC))

            gate_up(FFN1, act_hi, act_lo)

            def down(first):
                for j in range(2):
                    g = first + j
                    pe.wait_ge(taken, taken_before(g))
                    steps(g, 0, 4, ffn_hi, ffn_lo)
                    if j == 0:
                        turn_group(g)
                        steps(g, 4, FC - 4, ffn_hi, ffn_lo)
                        pe.wait_ge(taken, taken_before(g) + 1)
                        steps(g, FC - 4, FC, ffn_hi, ffn_lo)
                    elif first == DOWN1:
                        turn_residual(g, 1)
                        steps(g, 4, FC, ffn_hi, ffn_lo)
                    else:
                        steps(g, 4, FC, ffn_hi, ffn_lo)

            down(DOWN1)

            def from_residual(g, number, hi, lo):
                pe.wait_ge(taken, taken_before(g))
                steps(g, 0, 4, hi, lo)
                turn_residual(g, number)
                steps(g, 4, 8, hi, lo)
                pe.wait_ge(taken, taken_before(g) + 2)
                steps(g, 8, DC, hi, lo)

            from_residual(MIX_HB, 2, act_hi, act_lo)
            for g in range(MIX_HB + 1, MEM_K):
                pe.wait_ge(taken, taken_before(g))
                if g >= MIX_HB + 2:
                    pe.wait_ge(copied, g - MIX_HB - 1)
                steps(g, 0, 4, act_hi, act_lo)
                turn_group(g)
                steps(g, 4, 5, act_hi, act_lo)
                if g in MEM_ROUNDS:
                    pe.wait_ge(mem_in, 16 * HALVES)
                    turn_round(g, 1, of_rows(mem_raw, MEM_ROUNDS[g][0]))
                    steps(g, 5, 7, act_hi, act_lo)
                    pe.wait_ge(copied, g - MIX_HB)
                    turn_round(g, 2, of_rows(mem_raw, MEM_ROUNDS[g][1]))
                    steps(g, 7, DC, act_hi, act_lo)
                else:
                    steps(g, 5, DC, act_hi, act_lo)
            for g in range(MEM_K, MIX_OUT):
                pe.wait_ge(taken, taken_before(g))
                if g == MEM_K:
                    pe.wait_ge(copied, 4)
                steps(g, 0, 4, mem_hi, mem_lo)
                if g <= MEM_V:
                    turn_group(g)
                    steps(g, 4, DC, mem_hi, mem_lo)
                else:
                    pe.wait_ge(drained, drains_before(MEM_V) + 1)
                    pe.wait_ge(conv_b_ops, CONV_B_OPS)
                    for c in range(8):
                        last = nc.tensor.matmul(round_banks(g, 0)[:, 0, :], ones[:, :], conv_b[:, c, :],
                                                start=c == 0, stop=c == 7)
                    last.then_inc(ln_sum, 1)
                    steps(g, 4, 7, mem_hi, mem_lo)
                    pe.wait_ge(ln_square, 1)
                    for c in range(8):
                        last = nc.tensor.matmul(round_banks(g, 1)[:, 0, :], ones[:, :], squares[:, c, :],
                                                start=c == 0, stop=c == 7)
                    last.then_inc(ln_sum, 1)
                    steps(g, 7, DC, mem_hi, mem_lo)
            g = MIX_OUT
            pe.wait_ge(ln_var, 1)
            pe.wait_ge(y_ready, 1)
            steps(g, 0, 8, act_hi, act_lo)
            pe.wait_ge(y_ready, 2)
            steps(g, 8, DC, act_hi, act_lo)
            g = MIX_OUT + 1
            pe.wait_ge(drained, drains_before(MIX_OUT))
            steps(g, 0, 4, act_hi, act_lo)
            turn_residual(g, 3)
            steps(g, 4, DC, act_hi, act_lo)
            from_residual(MEM_Q, 4, uq_hi, uq_lo)

            def attend_scores(g, pair):
                for head in range(2):
                    for t in range(HALVES):
                        tokens = slice(t * P, (t + 1) * P)
                        n = 0
                        for a, b in ((act_hi, k_hi), (act_hi, k_lo), (act_lo, k_hi)):
                            for c in range(HC):
                                chunk = (2 * pair + head) * HC + c
                                last = nc.tensor.matmul(round_banks(g, 0)[:, 2 * head + t, :],
                                                        a[:, chunk, tokens], b[:, chunk, :],
                                                        start=n == 0, stop=n == 3 * HC - 1)
                                n += 1
                last.then_inc(scores_ready, 1)

            def attend_values(g, pair, head):
                for c in range(HC):
                    cols = slice((head * HC + c) * P, (head * HC + c + 1) * P)
                    n = 0
                    for a, b in ((v_hi, p_hi), (v_lo, p_hi), (v_hi, p_lo)):
                        for m in range(HALVES):
                            last = nc.tensor.matmul(round_banks(g, head)[:, c, :], a[pair][:, m, cols],
                                                    b[:, 2 * head + m, :],
                                                    start=n == 0, stop=n == 3 * HALVES - 1)
                            n += 1
                last.then_inc(turned, 1)

            for g, hi, lo, at in ((MEM_O - 1, uq_hi, uq_lo, (4, 7, 10, 13)),
                                  (MEM_O, k_hi, k_lo, (3, 4, 6, 7))):
                pair = ATTN[g]
                before = taken_before(g)
                pe.wait_ge(taken, before)
                steps(g, 0, at[0], hi, lo)
                turn_group(g)
                steps(g, at[0], at[1], hi, lo)
                pe.wait_ge(taken, before + 2)
                attend_scores(g, pair)
                steps(g, at[1], at[2], hi, lo)
                pe.wait_ge(p_ready, pair + 1)
                turn_round(g, 1, lambda c, t: gated[:, c // 2 * 2 + t, c % 2 * P:(c % 2 + 1) * P])
                steps(g, at[2], at[3], hi, lo)
                pe.wait_ge(taken, before + 3)
                for head in range(2):
                    attend_values(g, pair, head)
                if pair == 0:
                    steps(g, at[3], DC, hi, lo)
                else:
                    steps(g, at[3], 8, hi, lo)
                    pe.wait_ge(taken, before + 5)
                    steps(g, 8, DC, hi, lo)
            g = MEM_O + 1
            pe.wait_ge(taken, taken_before(g))
            steps(g, 0, 4, k_hi, k_lo)
            turn_residual(g, 5)
            steps(g, 4, DC, k_hi, k_lo)
            from_residual(FFN2, 6, act_hi, act_lo)
            gate_up(FFN2, act_hi, act_lo)
            down(DOWN2)


def _param_loads():
    row, loads = 0, 0
    for _, n in PARAMS:
        loads += 1 + (row % P + n - 1) // P
        row += n
    return loads


PARAM_LOADS = _param_loads()

_INS = ["x", "mem", "ffn1_norm", "ffn1_w_gate_up", "ffn1_w_down", "mix_norm", "w_mix_in", "conv_a_w",
        "conv_b_w", "conv_b_bias", "ln_b_gain", "ln_b_bias", "w_mix_out", "mem_q_norm",
        "mem_kv_norm", "w_mem_q", "w_mem_kv", "w_mem_o", "ffn2_norm", "ffn2_w_gate_up",
        "ffn2_w_down", "final_norm"]


def kernel(**inputs):
    import numpy as _np
    import concourse.bacc as _bacc
    from concourse import mybir as _mybir
    from concourse.bass_utils import run_bass_kernel_spmd as _run

    nc = _bacc.Bacc("TRN2", target_bir_lowering=False, num_devices=1, dynamic_dma_scratch_size=512)
    arrays, args = {}, []
    for name in _INS:
        a = _np.ascontiguousarray(inputs[name])
        arrays[f"in_{name}_dram"] = a
        args.append(nc.dram_tensor(f"in_{name}_dram", a.shape, _mybir.dt.from_np(a.dtype),
                                   kind="ExternalInput").ap())
    args.append(nc.dram_tensor("out_dram", (1, TOKENS, D), _mybir.dt.float32,
                               kind="ExternalOutput").ap())
    block_program(nc, *args)
    r = _run(nc, [arrays], core_ids=[0])
    return r.results[0]["out_dram"]
```

```python
import concourse.bass as bass
from concourse import mybir
from contextlib import ExitStack

P = 128
TOKENS = 256
HALVES = TOKENS // P
D = 2048
DC = D // P
FF = 5632
FC = FF // P
CA = D // 2
CB = D - CA
KS, KC = 3, 31
HEADS = 4
HD = D // HEADS
HC = HD // P
RMS_EPS, LN_EPS = 1e-6, 1e-5
SEG = 512
COLS = 2 * SEG
RAW, RING = 8, 4
AHEAD = 3

GU = FF // SEG
FFN1 = 0
DOWN1 = FFN1 + GU
MIX_HB = DOWN1 + 2
MIX_CX = MIX_HB + 2
MIX_BG = MIX_CX + 2
MEM_K = MIX_BG + 1
MEM_V = MEM_K + 2
MIX_OUT = MEM_V + 2
MEM_Q = MIX_OUT + 2
MEM_O = MEM_Q + 2
FFN2 = MEM_O + 2
DOWN2 = FFN2 + GU
GROUPS = DOWN2 + 2
NSTEPS = [FC if DOWN1 <= g < DOWN1 + 2 or g >= DOWN2 else DC for g in range(GROUPS)]
BASE = [sum(NSTEPS[:g]) for g in range(GROUPS + 1)]

X_ROUNDS = DC // 4
FIRST_STEPS = ((0, 1), (1, 3), (3, 4), (4, 5))
PARAM_ROUNDS = 2


def rounds_of(g):
    if g >= DOWN2 or MEM_V <= g < MIX_OUT:
        return 0
    if g < DOWN1 or FFN2 <= g or MIX_HB <= g < MIX_BG:
        return 1
    return 2


MEM_ROUNDS = {MIX_CX: (0, 1), MIX_CX + 1: (2, 3)}
ATTN = {MEM_O - 1: 0, MEM_O: 1}
ATTN_ROUNDS = 3


def turned_before(g):
    n = X_ROUNDS + PARAM_ROUNDS
    for at in range(1, g):
        n += rounds_of(at - 1) + len(MEM_ROUNDS.get(at, ())) + (ATTN_ROUNDS if at in ATTN else 0)
    return n


def copied_rounds(g):
    return MIX_HB <= g < MIX_BG


def taken_before(g):
    n = X_ROUNDS
    for at in range(1, g):
        n += (0 if copied_rounds(at - 1) else rounds_of(at - 1)) + len(MEM_ROUNDS.get(at, ()))
        n += ATTN_ROUNDS if at in ATTN else 0
    return n


def highs_before(g):
    return taken_before(g) - (2 if g > MIX_BG + 1 else 0)


def paired(g):
    return g < DOWN1 or MIX_HB <= g < MIX_BG or FFN2 <= g < DOWN2


def gated_before(g):
    return 2 * sum(paired(at) for at in range(g))


PARAMS = [("ffn1_norm", DC), ("mix_norm", DC), ("mem_q_norm", DC), ("mem_kv_norm", DC),
          ("ffn2_norm", DC), ("conv_b_bias", 8), ("ln_b_gain", 8), ("ln_b_bias", 8),
          ("conv_a_w", KS * 8), ("conv_b_w", KC * 8), ("conv_b_bias", 8)]
PCOL = {}
for _name, _n in PARAMS:
    PCOL.setdefault(_name, sum(n for _, n in PARAMS[:len(PCOL)]))
PTILES = 3
assert sum(n for _, n in PARAMS) == PTILES * P

TAPS = 3
CONV_B_OPS = 8 * KC
ST_FFN1, ST_MIX, ST_MEM, ST_Q, ST_FFN2, ST_FINAL = range(6)


def block_program(nc, x, mem, ffn1_norm, ffn1_w_gate_up, ffn1_w_down, mix_norm, w_mix_in, conv_a_w,
                  conv_b_w, conv_b_bias, ln_b_gain, ln_b_bias, w_mix_out, mem_q_norm, mem_kv_norm,
                  w_mem_q, w_mem_kv, w_mem_o, ffn2_norm, ffn2_w_gate_up, ffn2_w_down, final_norm,
                  out):
    f32, f32r = mybir.dt.float32, mybir.dt.float32r
    ALU, ACT, AX = mybir.AluOpType, mybir.ActivationFunctionType, mybir.AxisListType
    params = dict(ffn1_norm=ffn1_norm, mix_norm=mix_norm, mem_q_norm=mem_q_norm,
                  mem_kv_norm=mem_kv_norm, ffn2_norm=ffn2_norm, conv_b_bias=conv_b_bias,
                  ln_b_gain=ln_b_gain, ln_b_bias=ln_b_bias, conv_a_w=conv_a_w, conv_b_w=conv_b_w)

    def weights_of(g):
        if g < DOWN1:
            return ffn1_w_gate_up[0], g * SEG, FF + g * SEG
        if g < MIX_HB:
            w, c = ffn1_w_down[0], (g - DOWN1) * COLS
        elif g < MIX_CX:
            c = 3 * CA + (g - MIX_HB) * SEG
            return w_mix_in[0], c, c + CB
        elif g < MIX_BG:
            c = CA + (g - MIX_CX) * SEG
            return w_mix_in[0], c, c + CA
        elif g < MEM_K:
            w, c = w_mix_in[0], 0
        elif g < MIX_OUT:
            w, c = w_mem_kv[0], (g - MEM_K) * COLS
        elif g < MEM_Q:
            w, c = w_mix_out[0], (g - MIX_OUT) * COLS
        elif g < MEM_O:
            w, c = w_mem_q[0], (g - MEM_Q) * COLS
        elif g < FFN2:
            w, c = w_mem_o[0], (g - MEM_O) * COLS
        elif g < DOWN2:
            return ffn2_w_gate_up[0], (g - FFN2) * SEG, FF + (g - FFN2) * SEG
        else:
            w, c = ffn2_w_down[0], (g - DOWN2) * COLS
        return w, c, c + SEG

    ctx = ExitStack()
    with ctx:
        def sb(name, shape, dt=f32):
            return ctx.enter_context(nc.sbuf_tensor(name, shape, dt))

        def sem(name):
            return ctx.enter_context(nc.semaphore(name))

        h = sb("h", [P, HALVES, D])
        act_hi = sb("act_hi", [P, DC, TOKENS], f32r)
        act_lo = sb("act_lo", [P, DC, TOKENS], f32r)
        raw = sb("raw", [P, RAW, COLS])
        w_hi = sb("w_hi", [P, RING, COLS], f32r)
        w_lo = sb("w_lo", [P, RING, COLS], f32r)
        gated = sb("gated", [P, 4, 256])
        identity = sb("identity", [P, P])
        ones = sb("ones", [P, P])
        pcol = sb("pcol", [P, PTILES * P])
        ssq = sb("ssq", [P, 6, 2, HALVES])
        ssq_tail = sb("ssq_tail", [P, 2, HALVES])
        var = sb("var", [P, 6, HALVES])
        root = sb("root", [P, 6, HALVES])
        newton = sb("newton", [P, 6, HALVES])
        rstd = sb("rstd", [P, 6, HALVES])
        smax = sb("smax", [P, 4])
        nmax = sb("nmax", [P, 4])
        psum_p = sb("psum_p", [P, 4])
        rsum_p = sb("rsum_p", [P, 4])

        with nc.sbuf_tensor("tok", [P, HALVES, COLS], f32) as tok:
            pass
        with nc.sbuf_tensor("p_hi", [P, 4, TOKENS], f32r) as p_hi, \
                nc.sbuf_tensor("p_lo", [P, 4, TOKENS], f32r) as p_lo:
            pass
        tok_place = sb("tok_place", [P, HALVES * COLS])
        first_rows = tok[0:DC, 1, 0:P]
        param_rows = tok[:, 0, 0:PTILES * P].rearrange("p (t n) -> p t n", t=PTILES)
        final_gain = tok[:, :, :].rearrange("p a n -> p (a n)")
        squares = tok[:, :, :].rearrange("p a (c t) -> p (a c) t", t=TOKENS)

        kb = 256
        with nc.sbuf_tensor("ffn_hi", [P, FC, TOKENS], f32r) as ffn_hi, \
                nc.sbuf_tensor("ffn_lo", [P, FC, TOKENS], f32r) as ffn_lo:
            pass
        with nc.sbuf_tensor("mem_hi", [P, DC, TOKENS], f32r) as mem_hi, \
                nc.sbuf_tensor("mem_lo", [P, DC, TOKENS], f32r) as mem_lo, \
                nc.sbuf_tensor("k_hi", [P, DC, TOKENS], f32r) as k_hi, \
                nc.sbuf_tensor("k_lo", [P, DC, TOKENS], f32r) as k_lo, \
                nc.sbuf_tensor("v_hi0", [P, HALVES, COLS], f32r) as v_hi0, \
                nc.sbuf_tensor("v_lo0", [P, HALVES, COLS], f32r) as v_lo0, \
                nc.sbuf_tensor("v_hi1", [P, HALVES, COLS], f32r) as v_hi1, \
                nc.sbuf_tensor("v_lo1", [P, HALVES, COLS], f32r) as v_lo1:
            v_hi, v_lo = (v_hi0, v_hi1), (v_lo0, v_lo1)
        with nc.sbuf_tensor("uq_hi", [P, DC, TOKENS], f32r) as uq_hi, \
                nc.sbuf_tensor("uq_lo", [P, DC, TOKENS], f32r) as uq_lo, \
                nc.sbuf_tensor("mem_raw", [P, HALVES, D], f32) as mem_raw:
            pass
        with nc.sbuf_tensor("place0", [P, 64 * kb], f32), \
                nc.sbuf_tensor("hb", [P, 8, KC - 1 + TOKENS], f32) as hb, \
                nc.sbuf_tensor("cx", [P, 4, KS - 1 + TOKENS], f32) as cx:
            pass
        with nc.sbuf_tensor("place1", [P, 80 * kb], f32), \
                nc.sbuf_tensor("conv_b", [P, 8, TOKENS], f32) as conv_b, \
                nc.sbuf_tensor("conv_a", [P, 8, TOKENS], f32) as conv_a:
            pass
        sb("large_place", [P, 96 * kb])

        banks = ctx.enter_context(nc.psum_tensor("banks", [P, 2, HALVES, 2, SEG], f32))

        landed = [sem(f"landed{n}") for n in range(RAW // 2)]
        hi_ready = sem("hi_ready")
        lo_ready = sem("lo_ready")
        steps_done = sem("steps_done")
        params_in = sem("params_in")
        first_in = sem("first_in")
        x_in = [sem(f"x_in{r}") for r in range(X_ROUNDS)]
        mem_in = sem("mem_in")
        consts_ready = sem("consts_ready")
        const_zero = sem("const_zero")
        pcol_ready = sem("pcol_ready")
        pads_ready = sem("pads_ready")
        gated_ready = sem("gated_ready")
        drained = sem("drained")
        turned = sem("turned")
        high_made = sem("high_made")
        v_high_made = sem("v_high_made")
        taken = sem("taken")
        copied = sem("copied")
        h_ready = sem("h_ready")
        ssq_ready = sem("ssq_ready")
        var_ready = sem("var_ready")
        root_ready = sem("root_ready")
        rstd_ready = sem("rstd_ready")
        dve_chain = sem("dve_chain")
        conv_b_ops = sem("conv_b_ops")
        conv_a_ops = sem("conv_a_ops")
        ya_high = sem("ya_high")
        y_ready = sem("y_ready")
        ln_chunks = sem("ln_chunks")
        ln_sum = sem("ln_sum")
        ln_diff = sem("ln_diff")
        ln_square = sem("ln_square")
        ln_var = sem("ln_var")
        ln_root = sem("ln_root")
        ln_normed = sem("ln_normed")
        yb_ready = sem("yb_ready")
        yb_high = sem("yb_high")
        scores_ready = sem("scores_ready")
        nmax_ready = sem("nmax_ready")
        exp_ready = sem("exp_ready")
        p_ready = sem("p_ready")
        final_gain_in = sem("final_gain_in")
        half_done = sem("half_done")
        tail_added = sem("tail_added")
        tail_ssq = sem("tail_ssq")
        tail_gained = sem("tail_gained")
        out_ready_act = sem("out_ready_act")
        out_ready_dve = sem("out_ready_dve")
        out_stored = sem("out_stored")

        block = ctx.enter_context(nc.Block())

        def round_banks(g, r):
            return banks[:, (g + 1) % 2, r % 2, :, :].rearrange("p s (c t) -> p (s c) t", t=TOKENS)

        @block.sync
        def _(sp):
            def load_steps(g, k, base, shift=0, wait=True):
                n = BASE[g] + k
                slot = n % RAW
                if wait:
                    sp.wait_ge(lo_ready, base + (k + 2 - RAW))
                w, c0, c1 = weights_of(g)
                c0, c1 = c0 + shift, c1 + shift
                for s, c in enumerate((c0, c1)):
                    rows = w[k * P:(k + 2) * P, bass.ds(c, SEG)].rearrange("(a p) n -> p a n", p=P)
                    sp.dma_start(raw[:, slot:slot + 2, s * SEG:(s + 1) * SEG], rows) \
                      .then_inc(landed[slot // 2], 16)

            def load_wide(g, k):
                n = BASE[g] + k
                slot = n % RAW
                sp.wait_ge(lo_ready, n + 2 - RAW)
                w, c0, _ = weights_of(g)
                for a in range(2):
                    sp.dma_start(raw[:, slot + a, :], w[(k + a) * P:(k + a + 1) * P, c0:c0 + COLS]) \
                      .then_inc(landed[slot // 2], 16)

            sp.dma_start(first_rows, ffn1_norm[0].rearrange("(c p) -> c p", p=P)).then_inc(first_in, 16)
            for r in range(X_ROUNDS):
                for t in range(HALVES):
                    cols = slice(r * SEG, (r + 1) * SEG)
                    sp.dma_start(h[:, t, cols], x[0, t * P:(t + 1) * P, cols]).then_inc(x_in[r], 16)
                if r % 2 == 1:
                    load_steps(FFN1, r - 1, 0, wait=False)

            def load_params():
                row = 0
                for name, n in PARAMS:
                    v = params[name][0]
                    v = v.rearrange("k (c p) -> (k c) p", p=P) if len(v.shape) == 2 else \
                        v.rearrange("(c p) -> c p", p=P)
                    done = 0
                    while done < n:
                        m = min(n - done, P - row % P)
                        sp.dma_start(param_rows[row % P:row % P + m, row // P, :],
                                     v[done:done + m, :]).then_inc(params_in, 16)
                        done += m
                        row += m

            def gate_up(first):
                for k in range(4 if first == FFN1 else 0, DC, 2):
                    load_steps(first, k, BASE[first], wait=BASE[first] + k >= RAW)
                    if first == FFN1 and k == RAW:
                        load_params()
                with sp.Fori(0, (GU - 1) // 2) as i:
                    for j in range(2):
                        for k in range(0, DC, 2):
                            load_steps(first + 1 + j, k, BASE[first + 1 + j] + i * (2 * DC),
                                       shift=i * (2 * SEG))

            gate_up(FFN1)
            for g in range(DOWN1, FFN2):
                for k in range(0, NSTEPS[g], 2):
                    if g == MIX_HB and k == 8:
                        sp.wait_ge(steps_done, BASE[MIX_HB])
                        for t in range(HALVES):
                            sp.dma_start(mem_raw[:, t, :], mem[0, t * P:(t + 1) * P, :]) \
                              .then_inc(mem_in, 16)
                    if MIX_HB <= g < MIX_BG:
                        load_steps(g, k, BASE[g])
                    else:
                        load_wide(g, k)
            gate_up(FFN2)
            for g in range(DOWN2, GROUPS):
                for k in range(0, NSTEPS[g], 2):
                    load_wide(g, k)
                    if g == DOWN2 and k == 16:
                        sp.wait_ge(turned, turned_before(DOWN2 + 1))
                        sp.dma_start(final_gain, final_norm.rearrange("(a n) -> a n", a=1)
                                     .partition_broadcast(P)).then_inc(final_gain_in, 16)
            for t in range(HALVES):
                for ready, c in ((out_ready_act, 0), (out_ready_dve, COLS)):
                    sp.wait_ge(ready, t + 1)
                    sp.dma_start(out[0, t * P:(t + 1) * P, c:c + COLS], h[:, t, c:c + COLS]) \
                      .then_inc(out_stored, 16)
            sp.wait_ge(out_stored, 16 * 2 * HALVES)

        @block.gpsimd
        def _(pool):
            nc.gpsimd.memset(ones[:, :], 1.0).then_inc(consts_ready, 1)
            nc.gpsimd.memset(identity[:, :], 0.0).then_inc(const_zero, 1)
            pool.wait_ge(const_zero, 1)
            nc.gpsimd.affine_select(out=identity[:, :], in_=identity[:, :],
                                    compare_op=ALU.not_equal, fill=1.0, base=0,
                                    pattern=[[-1, P]], channel_multiplier=1).then_inc(consts_ready, 1)
            pool.wait_ge(steps_done, BASE[MIX_HB])
            nc.gpsimd.memset(hb[:, :, 0:KC - 1], 0.0).then_inc(pads_ready, 1)
            nc.gpsimd.memset(cx[:, :, 0:KS - 1], 0.0).then_inc(pads_ready, 1)

        @block.scalar
        def _(act):
            def highs(g, k0, k1, off=0):
                for k in range(k0, k1):
                    n = BASE[g] + k
                    act.wait_ge(landed[n % RAW // 2], (n // RAW + 1) * 32 + off * (32 // RAW))
                    if n >= RING:
                        act.wait_ge(steps_done, n + 1 - RING + off)
                    nc.scalar.activation(w_hi[:, n % RING, :], raw[:, n % RAW, :], ACT.Copy) \
                        .then_inc(hi_ready, 1)

            def high_round(g, r, dst, chunk, gain, number):
                act.wait_ge(turned, number)
                src = round_banks(g, r)
                if gain is None:
                    last = nc.scalar.activation(dst[:, bass.ds(chunk, 4), :], src, ACT.Copy)
                else:
                    for c in range(4):
                        col = PCOL[gain] + chunk + c
                        last = nc.scalar.activation(dst[:, chunk + c, :], src[:, c, :], ACT.Copy,
                                                    scale=pcol[:, col:col + 1])
                last.then_inc(high_made, 1)

            def gate(g, func, seg, stat, off=0):
                act.wait_ge(steps_done, BASE[g + 1] + off)
                act.wait_ge(rstd_ready, stat + 1)
                for t in range(HALVES):
                    nc.scalar.activation(gated[:, 2 * t:2 * t + 2, :].rearrange("p a n -> p (a n)"),
                                         banks[:, g % 2, t, seg, :], func,
                                         scale=rstd[:, stat, t:t + 1]).then_inc(gated_ready, 1)

            def drain_scaled(g, stat):
                act.wait_ge(steps_done, BASE[g + 1])
                act.wait_ge(rstd_ready, stat + 1)
                for t in range(HALVES):
                    for s in range(2):
                        last = nc.scalar.activation(tok[:, t, s * SEG:(s + 1) * SEG],
                                                    banks[:, g % 2, t, s, :], ACT.Copy,
                                                    scale=rstd[:, stat, t:t + 1])
                last.then_inc(drained, 1)

            def squares_of(src, stat, part, cols):
                for t in range(HALVES):
                    before = 4 * stat + 2 * part + t
                    if before:
                        act.wait_ge(ssq_ready, before)
                    nc.scalar.activation(tok_junk(cols), src[:, t, part * cols:(part + 1) * cols],
                                         ACT.Square, accum_out=ssq[:, stat, part, t:t + 1]) \
                        .then_inc(ssq_ready, 1)

            def tok_junk(cols):
                return gated[:, :, :].rearrange("p a n -> p (a n)")[:, 0:cols]

            def square_root(stat):
                act.wait_ge(var_ready, stat + 1)
                nc.scalar.activation(root[:, stat, :], var[:, stat, :], ACT.Sqrt) \
                    .then_inc(root_ready, 1)

            def residual_squares(g, part, stat):
                act.wait_ge(h_ready, 2 * stat_order.index(stat) + part + 1)
                squares_of(h, stat, part, COLS)

            stat_order = [ST_MIX, ST_Q, ST_FFN2, ST_FINAL]

            act.wait_ge(turned, 1)
            nc.scalar.activation(pcol[:, 0:DC], banks[:, 1, 0, 0, 0:DC], ACT.Copy) \
                .then_inc(pcol_ready, 1)
            act.wait_ge(pcol_ready, 1)
            for r, (k0, k1) in enumerate(FIRST_STEPS):
                high_round(FFN1, r, act_hi, 4 * r, "ffn1_norm", 2 + r)
                highs(FFN1, k0, k1)
            highs(FFN1, FIRST_STEPS[-1][1], 9)
            squares_of(h, ST_FFN1, 0, COLS)
            highs(FFN1, 9, 11)
            squares_of(h, ST_FFN1, 1, COLS)
            highs(FFN1, 11, 13)
            square_root(ST_FFN1)
            highs(FFN1, 13, DC)
            act.wait_ge(turned, 2 + X_ROUNDS)
            nc.scalar.activation(pcol[:, DC:], banks[:, 1, 0, 0, DC:PTILES * P], ACT.Copy) \
                .then_inc(pcol_ready, 1)
            act.wait_ge(pcol_ready, 2)

            def gate_up(first, stat):
                nc.scalar.preload_act_table(ACT.Silu)
                with act.Fori(0, (GU - 1) // 2) as i:
                    for j in range(2):
                        g = first + 1 + j
                        highs(g, 0, AHEAD, i * (2 * DC))
                        gate(g - 1, ACT.Silu, 0, stat, i * (2 * DC))
                        highs(g, AHEAD, 7, i * (2 * DC))
                        high_round(g, 0, ffn_hi, i * 8 + 4 * j, None, turned_before(g) + 1 + i * 2)
                        highs(g, 7, DC, i * (2 * DC))
                g = first + GU
                highs(g, 0, AHEAD)
                gate(g - 1, ACT.Silu, 0, stat)
                highs(g, AHEAD, 7)
                high_round(g, 0, ffn_hi, FC - 4, None, turned_before(g) + 1)
                long_highs(g, 7)

            def long_highs(g, k0):
                k1 = NSTEPS[g] - (NSTEPS[g] - k0) % RAW
                with act.Fori(0, (k1 - k0) // RAW) as i:
                    highs(g, k0, k0 + RAW, i * RAW)
                highs(g, k1, NSTEPS[g])

            gate_up(FFN1, ST_FFN1)

            def residual_group(g, part, stat, dst, gain):
                highs(g, 0, AHEAD)
                residual_squares(g - 1, part, stat)
                highs(g, AHEAD, 5)
                if part == 1:
                    square_root(stat)
                highs(g, 5, 7)
                for r in range(2):
                    high_round(g, r, dst, 8 * part + 4 * r, gain, turned_before(g) + 1 + r)

            residual_group(DOWN1 + 1, 0, ST_MIX, act_hi, "mix_norm")
            long_highs(DOWN1 + 1, 7)
            residual_group(MIX_HB, 1, ST_MIX, act_hi, "mix_norm")
            highs(MIX_HB, 7, DC)

            def copy_round(g, dst, pad, number):
                act.wait_ge(turned, number)
                nc.scalar.activation(dst[:, :, pad:pad + TOKENS], round_banks(g, 0), ACT.Copy) \
                    .then_inc(copied, 1)

            def mem_rounds(g):
                for m, r in enumerate(MEM_ROUNDS[g]):
                    high_round(g, m + 1, mem_hi, 4 * r, "mem_kv_norm", turned_before(g) + 2 + m)
                    highs(g, 8 + m, 9 + m)

            for j in range(2):
                g = MIX_HB + 1 + j
                highs(g, 0, AHEAD)
                gate(g - 1, ACT.Sigmoid, 1, ST_MIX)
                highs(g, AHEAD, 7)
                if j == 0:
                    act.wait_ge(pads_ready, 2)
                copy_round(g, hb[:, 4 * j:4 * j + 4, :], KC - 1, turned_before(g) + 1)
                highs(g, 7, 8)
                if j == 0:
                    act.wait_ge(mem_in, 32)
                    for part in range(2):
                        squares_of(mem_raw, ST_MEM, part, COLS)
                    highs(g, 8, 10)
                    square_root(ST_MEM)
                else:
                    mem_rounds(g)
                highs(g, 10, DC)
            for j in range(2):
                g = MIX_CX + 1 + j
                highs(g, 0, AHEAD)
                gate(g - 1, ACT.Copy, 0, ST_MIX)
                highs(g, AHEAD, 7)
                if j == 1:
                    act.wait_ge(conv_a_ops, 4 * KS)
                copy_round(g, cx[:, :, :], KS - 1, turned_before(g) + 1)
                highs(g, 7, 8)
                if g in MEM_ROUNDS:
                    mem_rounds(g)
                    highs(g, 10, DC)
                else:
                    highs(g, 8, DC)
            highs(MEM_K, 0, AHEAD)
            drain_scaled(MIX_BG, ST_MIX)
            highs(MEM_K, AHEAD, 8)
            act.wait_ge(taken, taken_before(MEM_K) + 2)
            nc.scalar.activation(act_hi[:, 0:8, :], conv_a[:, :, :], ACT.Copy).then_inc(ya_high, 1)
            highs(MEM_K, 8, DC)
            for j in range(2):
                g = MEM_K + 1 + j
                highs(g, 0, AHEAD)
                drain_scaled(g - 1, ST_MEM)
                highs(g, AHEAD, 7)
                for r in range(2):
                    high_round(g, r, k_hi, 8 * j + 4 * r, None, turned_before(g) + 1 + r)
                highs(g, 7, DC)

            def drain_v(j):
                act.wait_ge(steps_done, BASE[MEM_V + j + 1])
                if j == 0:
                    act.wait_ge(conv_b_ops, CONV_B_OPS)
                else:
                    act.wait_ge(y_ready, 2)
                for t in range(HALVES):
                    for s in range(2):
                        last = nc.scalar.activation(v_hi[j][:, t, s * SEG:(s + 1) * SEG],
                                                    banks[:, (MEM_V + j) % 2, t, s, :], ACT.Copy,
                                                    scale=rstd[:, ST_MEM, t:t + 1])
                last.then_inc(v_high_made, 1)

            g = MEM_V + 1
            highs(g, 0, AHEAD)
            drain_v(0)
            highs(g, AHEAD, 7)
            act.wait_ge(ln_diff, 1)
            nc.scalar.activation(squares, conv_b[:, :, :], ACT.Square).then_inc(ln_square, 1)
            highs(g, 7, 12)
            act.wait_ge(ln_var, 1)
            nc.scalar.activation(gated[:, 1, :], gated[:, 0, :], ACT.Sqrt).then_inc(ln_root, 1)
            nc.scalar.preload_act_table(ACT.Silu)
            highs(g, 12, 13)
            act.wait_ge(ln_normed, 1)
            for c in range(8):
                g1, b1 = PCOL["ln_b_gain"] + c, PCOL["ln_b_bias"] + c
                last = nc.scalar.activation(conv_b[:, c, :], conv_b[:, c, :], ACT.Silu,
                                            scale=pcol[:, g1:g1 + 1], bias=pcol[:, b1:b1 + 1])
                if c % 3 == 1:
                    highs(g, 13 + c // 3, 14 + c // 3)
            last.then_inc(yb_ready, 1)
            act.wait_ge(yb_ready, 1)
            nc.scalar.activation(act_hi[:, 8:16, :], conv_b[:, :, :], ACT.Copy).then_inc(yb_high, 1)
            highs(MIX_OUT, 0, AHEAD)
            drain_v(1)
            highs(MIX_OUT, AHEAD, DC)
            residual_group(MIX_OUT + 1, 0, ST_Q, uq_hi, "mem_q_norm")
            highs(MIX_OUT + 1, 7, DC)
            residual_group(MEM_Q, 1, ST_Q, uq_hi, "mem_q_norm")
            highs(MEM_Q, 7, DC)

            for g, at in ((MEM_O - 1, (6, 9, 12, 15)), (MEM_O, (5, 6, 8, 9))):
                pair = ATTN[g]
                number = turned_before(g)
                highs(g, 0, AHEAD)
                drain_scaled(g - 1, ST_Q)
                highs(g, AHEAD, at[0])
                for r in range(2):
                    high_round(g, r, act_hi, 8 * pair + 4 * r, None, number + 1 + r)
                highs(g, at[0], at[1])
                act.wait_ge(nmax_ready, pair + 1)
                for n in range(4):
                    nc.scalar.activation(gated[:, n, :], round_banks(g, 0)[:, n, :], ACT.Exp,
                                         bias=nmax[:, n:n + 1], scale=float(HD) ** -0.5,
                                         accum_out=psum_p[:, n:n + 1]).then_inc(exp_ready, 1)
                highs(g, at[1], at[2])
                high_round(g, 1, p_hi, 0, None, number + 3)
                highs(g, at[2], at[3])
                for r in range(2):
                    high_round(g, r, k_hi, 8 * pair + 4 * r, None, number + 4 + r)
                highs(g, at[3], DC)
            residual_group(MEM_O + 1, 0, ST_FFN2, act_hi, "ffn2_norm")
            highs(MEM_O + 1, 7, DC)
            residual_group(FFN2, 1, ST_FFN2, act_hi, "ffn2_norm")
            highs(FFN2, 7, DC)
            gate_up(FFN2, ST_FFN2)
            g = DOWN2 + 1
            highs(g, 0, AHEAD)
            residual_squares(DOWN2, 0, ST_FINAL)
            nc.scalar.preload_act_table(ACT.Sqrt)
            long_highs(g, AHEAD)
            for t in range(HALVES):
                for s in range(2):
                    n = 2 * t + s
                    act.wait_ge(tail_added, n + 1)
                    c = COLS + s * SEG
                    nc.scalar.activation(gated[:, 2 * (n % 2):2 * (n % 2) + 2, :], h[:, t, c:c + SEG]
                                         .rearrange("p (a n) -> p a n", a=2), ACT.Square,
                                         accum_out=ssq_tail[:, s, t:t + 1]).then_inc(tail_ssq, 1)
                    if n >= 1:
                        act.wait_ge(tail_ssq, n)
            square_root(ST_FINAL)
            act.wait_ge(rstd_ready, ST_FINAL + 1)
            act.wait_ge(tail_gained, 1)
            for t in range(HALVES):
                nc.scalar.activation(h[:, t, 0:COLS], h[:, t, 0:COLS], ACT.Copy,
                                     scale=rstd[:, ST_FINAL, t:t + 1]).then_inc(out_ready_act, 1)

        @block.vector
        def _(dve):
            chain = [0]

            def link(instruction):
                chain[0] += 1
                instruction.then_inc(dve_chain, 1)
                dve.wait_ge(dve_chain, chain[0])

            def lows(g, k0, k1, off=0):
                for k in range(k0, k1):
                    n = BASE[g] + k
                    dve.wait_ge(hi_ready, n + 1 + off)
                    nc.vector.tensor_tensor(w_lo[:, n % RING, :], raw[:, n % RAW, :],
                                            w_hi[:, n % RING, :].bitcast(f32), ALU.subtract) \
                        .then_inc(lo_ready, 1)

            def long_lows(g, k0):
                k1 = NSTEPS[g] - (NSTEPS[g] - k0) % RAW
                with dve.Fori(0, (k1 - k0) // RAW) as i:
                    lows(g, k0, k0 + RAW, i * RAW)
                lows(g, k1, NSTEPS[g])

            def low_round(g, r, hi, lo, chunk, gain, number):
                dve.wait_ge(high_made, number)
                src = round_banks(g, r)
                if gain is None:
                    for s in range(2):
                        c = bass.ds(chunk + 2 * s, 2)
                        last = nc.vector.tensor_tensor(lo[:, c, :], src[:, 2 * s:2 * s + 2, :],
                                                       hi[:, c, :].bitcast(f32), ALU.subtract)
                else:
                    for c in range(4):
                        col = PCOL[gain] + chunk + c
                        last = nc.vector.scalar_tensor_tensor(
                            out=lo[:, chunk + c, :], in0=src[:, c, :], scalar=pcol[:, col:col + 1],
                            in1=hi[:, chunk + c, :].bitcast(f32), op0=ALU.mult, op1=ALU.subtract)
                last.then_inc(taken, 1)

            def drain_gated(g, seg, stat, number):
                for t in range(HALVES):
                    dve.wait_ge(gated_ready, number + t + 1)
                    last = nc.vector.scalar_tensor_tensor(
                        out=tok[:, t, 0:SEG], in0=banks[:, g % 2, t, seg, :],
                        scalar=rstd[:, stat, t:t + 1],
                        in1=gated[:, 2 * t:2 * t + 2, :].rearrange("p a n -> p (a n)"),
                        op0=ALU.mult, op1=ALU.mult)
                last.then_inc(drained, 1)

            def add_residual(g, part, factor):
                dve.wait_ge(steps_done, BASE[g + 1])
                for t in range(HALVES):
                    for s in range(2):
                        cols = h[:, t, part * COLS + s * SEG:part * COLS + (s + 1) * SEG]
                        last = nc.vector.scalar_tensor_tensor(
                            out=cols, in0=banks[:, g % 2, t, s, :], scalar=factor, in1=cols,
                            op0=ALU.mult, op1=ALU.add)
                last.then_inc(h_ready, 1)

            def norm_factor(stat, number, sums=4):
                dve.wait_ge(ssq_ready, 4 * number + sums)
                link(nc.vector.tensor_tensor(var[:, stat, :], ssq[:, stat, 0, :], ssq[:, stat, 1, :],
                                             ALU.add))
                nc.vector.tensor_scalar(var[:, stat, :], var[:, stat, :], 1.0 / D, RMS_EPS,
                                        ALU.mult, ALU.add).then_inc(var_ready, 1)
                dve.wait_ge(root_ready, number + 1)
                rsqrt(rstd[:, stat, :], var[:, stat, :], root[:, stat, :], newton[:, stat, :],
                      rstd_ready)

            def rsqrt(out_, a, sqrt_a, tmp, done):
                link(nc.vector.reciprocal(out_, sqrt_a))
                link(nc.vector.tensor_tensor(tmp, out_, out_, ALU.mult))
                link(nc.vector.tensor_tensor(tmp, tmp, a, ALU.mult))
                link(nc.vector.tensor_scalar(tmp, tmp, -0.5, 1.5, ALU.mult, ALU.add))
                nc.vector.tensor_tensor(out_, out_, tmp, ALU.mult).then_inc(done, 1)

            def conv_b_taps(first, count):
                for n in range(first, min(first + count, CONV_B_OPS)):
                    c, tap = n // (4 * KC) * 4 + n % 4, n % (4 * KC) // 4
                    w = PCOL["conv_b_w"] + tap * 8 + c
                    src = hb[:, c, tap:tap + TOKENS]
                    if tap == 0:
                        b = PCOL["conv_b_bias"] + c
                        ins = nc.vector.tensor_scalar(conv_b[:, c, :], src, pcol[:, w:w + 1],
                                                      pcol[:, b:b + 1], ALU.mult, ALU.add)
                    else:
                        dve.wait_ge(conv_b_ops, n - 3)
                        ins = nc.vector.scalar_tensor_tensor(
                            out=conv_b[:, c, :], in0=src, scalar=pcol[:, w:w + 1],
                            in1=conv_b[:, c, :], op0=ALU.mult, op1=ALU.add)
                    ins.then_inc(conv_b_ops, 1)

            def conv_a_tap(part, tap):
                for c4 in range(4):
                    c = 4 * part + c4
                    w = PCOL["conv_a_w"] + tap * 8 + c
                    src = cx[:, c4, tap:tap + TOKENS]
                    if tap == 0:
                        ins = nc.vector.tensor_scalar(conv_a[:, c, :], src, pcol[:, w:w + 1], None,
                                                      ALU.mult)
                    else:
                        dve.wait_ge(conv_a_ops, part * 4 * KS + 4 * tap + c4 - 3)
                        ins = nc.vector.scalar_tensor_tensor(
                            out=conv_a[:, c, :], in0=src, scalar=pcol[:, w:w + 1],
                            in1=conv_a[:, c, :], op0=ALU.mult, op1=ALU.add)
                    ins.then_inc(conv_a_ops, 1)

            for r, (k0, k1) in enumerate(FIRST_STEPS):
                low_round(FFN1, r, act_hi, act_lo, 4 * r, "ffn1_norm", r + 1)
                lows(FFN1, k0, k1)
            lows(FFN1, FIRST_STEPS[-1][1], 13)
            norm_factor(ST_FFN1, 0)
            lows(FFN1, 13, DC)
            dve.wait_ge(pcol_ready, 2)

            def gate_up(first, stat, order):
                dve.wait_ge(rstd_ready, order + 1)
                with dve.Fori(0, (GU - 1) // 2) as i:
                    for j in range(2):
                        g = first + 1 + j
                        lows(g, 0, AHEAD, i * (2 * DC))
                        drain_gated(g - 1, 1, stat, gated_before(g - 1) + i * 4)
                        lows(g, AHEAD, 7, i * (2 * DC))
                        low_round(g, 0, ffn_hi, ffn_lo, i * 8 + 4 * j, None,
                                  highs_before(g) + 1 + i * 2)
                        lows(g, 7, DC, i * (2 * DC))
                g = first + GU
                lows(g, 0, AHEAD)
                drain_gated(g - 1, 1, stat, gated_before(g - 1))
                lows(g, AHEAD, 7)
                low_round(g, 0, ffn_hi, ffn_lo, FC - 4, None, highs_before(g) + 1)
                long_lows(g, 7)

            gate_up(FFN1, ST_FFN1, 0)

            def residual_group(g, part, factor, stat, order, hi, lo, gain):
                lows(g, 0, AHEAD)
                add_residual(g - 1, part, factor)
                lows(g, AHEAD, 5)
                if part == 1:
                    norm_factor(stat, order)
                lows(g, 5, 7)
                for r in range(2):
                    low_round(g, r, hi, lo, 8 * part + 4 * r, gain,
                              highs_before(g) + 1 + r)

            residual_group(DOWN1 + 1, 0, 0.5, ST_MIX, 1, act_hi, act_lo, "mix_norm")
            long_lows(DOWN1 + 1, 7)
            residual_group(MIX_HB, 1, 0.5, ST_MIX, 1, act_hi, act_lo, "mix_norm")
            lows(MIX_HB, 7, DC)

            g = MIX_HB + 1
            lows(g, 0, AHEAD)
            drain_gated(g - 1, 0, ST_MIX, gated_before(g - 1))
            lows(g, AHEAD, 10)
            norm_factor(ST_MEM, 2)
            dve.wait_ge(copied, 1)
            op = 0
            for k in range(10, DC):
                lows(g, k, k + 1)
                conv_b_taps(op, TAPS)
                op += TAPS
            for g in range(MIX_CX, MEM_V + 1):
                for k in range(AHEAD):
                    lows(g, k, k + 1)
                    conv_b_taps(op, TAPS)
                    op += TAPS
                if g <= MIX_BG:
                    drain_gated(g - 1, 0 if g == MIX_CX else 1, ST_MIX, gated_before(g - 1))
                for k in range(AHEAD, 8):
                    lows(g, k, k + 1)
                    if k < 7 and (g not in MEM_ROUNDS or k < 4):
                        conv_b_taps(op, TAPS)
                        op += TAPS
                if g == MIX_CX:
                    dve.wait_ge(copied, 2)
                if g == MEM_K:
                    dve.wait_ge(conv_a_ops, 2 * 4 * KS)
                    for r in range(2):
                        dve.wait_ge(turned, turned_before(g) + 1 + r)
                        chunks = conv_a[:, 4 * r:4 * r + 4, :]
                        for s in range(2):
                            part = chunks[:, 2 * s:2 * s + 2, :]
                            last = nc.vector.tensor_tensor(part, round_banks(g, r)[:, 2 * s:2 * s + 2, :],
                                                           part, ALU.mult)
                        last.then_inc(taken, 1)
                if g > MEM_K:
                    for r in range(2):
                        low_round(g, r, k_hi, k_lo, 8 * (g - MEM_K - 1) + 4 * r, None,
                                  highs_before(g) + 1 + r)
                for k in range(8, DC):
                    if g in MEM_ROUNDS and k in (8, 9):
                        m = k - 8
                        low_round(g, m + 1, mem_hi, mem_lo, 4 * MEM_ROUNDS[g][m], "mem_kv_norm",
                                  highs_before(g) + 1 + m)
                    lows(g, k, k + 1)
                    if g in (MIX_CX + 1, MIX_BG) and k < 8 + KS:
                        if k == 8:
                            dve.wait_ge(copied, 3 + g - MIX_CX - 1)
                        conv_a_tap(g - MIX_CX - 1, k - 8)
                    else:
                        conv_b_taps(op, TAPS)
                        op += TAPS
                    if g == MEM_K and k == 10:
                        dve.wait_ge(ya_high, 1)
                        nc.vector.tensor_tensor(act_lo[:, 0:8, :], conv_a[:, :, :],
                                                act_hi[:, 0:8, :].bitcast(f32), ALU.subtract) \
                            .then_inc(y_ready, 1)
            assert op >= CONV_B_OPS

            def drain_v(j):
                g = MEM_V + j
                dve.wait_ge(v_high_made, j + 1)
                for t in range(HALVES):
                    for s in range(2):
                        cols = slice(s * SEG, (s + 1) * SEG)
                        last = nc.vector.scalar_tensor_tensor(
                            out=v_lo[j][:, t, cols], in0=banks[:, g % 2, t, s, :],
                            scalar=rstd[:, ST_MEM, t:t + 1], in1=v_hi[j][:, t, cols].bitcast(f32),
                            op0=ALU.mult, op1=ALU.subtract)
                last.then_inc(drained, 1)

            g = MEM_V + 1
            sums = round_banks(g, 0)[:, 0, :]
            squared = round_banks(g, 1)[:, 0, :]
            dve.wait_ge(conv_b_ops, CONV_B_OPS)
            nc.vector.reduce_sum(gated[:, 3, :], conv_b[:, :, :].rearrange("p c t -> p t c"), AX.X) \
                .then_inc(ln_chunks, 1)
            lows(g, 0, AHEAD)
            drain_v(0)
            lows(g, AHEAD, 6)
            dve.wait_ge(ln_sum, 1)
            mean = gated[:, 2, :]
            link(nc.vector.tensor_scalar(mean, sums, 1.0 / CB, None, ALU.mult))
            nc.vector.tensor_tensor(conv_b[:, :, :], conv_b[:, :, :],
                                    mean.unsqueeze(1).to_broadcast([P, 8, TOKENS]), ALU.subtract) \
                .then_inc(ln_diff, 1)
            lows(g, 6, 8)
            dve.wait_ge(ln_square, 1)
            nc.vector.reduce_sum(gated[:, 3, :], squares.rearrange("p c t -> p t c"), AX.X) \
                .then_inc(ln_chunks, 1)
            lows(g, 8, 11)
            dve.wait_ge(ln_sum, 2)
            nc.vector.tensor_scalar(gated[:, 0, :], squared, 1.0 / CB, LN_EPS, ALU.mult, ALU.add) \
                .then_inc(ln_var, 1)
            lows(g, 11, 12)
            dve.wait_ge(ln_root, 1)
            rsqrt(gated[:, 2, :], gated[:, 0, :], gated[:, 1, :], gated[:, 3, :], ln_root)
            dve.wait_ge(ln_root, 2)
            nc.vector.tensor_tensor(conv_b[:, :, :], conv_b[:, :, :],
                                    gated[:, 2, :].unsqueeze(1).to_broadcast([P, 8, TOKENS]),
                                    ALU.mult).then_inc(ln_normed, 1)
            lows(g, 12, DC)
            dve.wait_ge(yb_high, 1)
            nc.vector.tensor_tensor(act_lo[:, 8:16, :], conv_b[:, :, :],
                                    act_hi[:, 8:16, :].bitcast(f32), ALU.subtract) \
                .then_inc(y_ready, 1)
            lows(MIX_OUT, 0, AHEAD)
            drain_v(1)
            lows(MIX_OUT, AHEAD, DC)
            residual_group(MIX_OUT + 1, 0, 1.0, ST_Q, 3, uq_hi, uq_lo, "mem_q_norm")
            lows(MIX_OUT + 1, 7, DC)
            residual_group(MEM_Q, 1, 1.0, ST_Q, 3, uq_hi, uq_lo, "mem_q_norm")
            lows(MEM_Q, 7, DC)

            for g, at in ((MEM_O - 1, (6, 9, 12, 15)), (MEM_O, (5, 6, 8, 9))):
                pair = ATTN[g]
                number = highs_before(g)
                lows(g, 0, at[0])
                for r in range(2):
                    low_round(g, r, act_hi, act_lo, 8 * pair + 4 * r, None, number + 1 + r)
                lows(g, at[0], at[1])
                dve.wait_ge(scores_ready, pair + 1)
                scores = round_banks(g, 0)
                for s in range(2):
                    last = nc.vector.reduce_max(smax[:, 2 * s:2 * s + 2], scores[:, 2 * s:2 * s + 2, :],
                                                AX.X)
                link(last)
                nc.vector.tensor_scalar(nmax[:, :], smax[:, :], -float(HD) ** -0.5, None, ALU.mult) \
                    .then_inc(nmax_ready, 1)
                dve.wait_ge(exp_ready, 4 * (pair + 1))
                link(nc.vector.reciprocal(rsum_p[:, :], psum_p[:, :]))
                for n in range(4):
                    last = nc.vector.tensor_scalar(gated[:, n, :], gated[:, n, :],
                                                   rsum_p[:, n:n + 1], None, ALU.mult)
                last.then_inc(p_ready, 1)
                lows(g, at[1], at[2])
                low_round(g, 1, p_hi, p_lo, 0, None, number + 3)
                lows(g, at[2], at[3])
                for r in range(2):
                    low_round(g, r, k_hi, k_lo, 8 * pair + 4 * r, None, number + 4 + r)
                lows(g, at[3], DC)
            residual_group(MEM_O + 1, 0, 1.0, ST_FFN2, 4, act_hi, act_lo, "ffn2_norm")
            lows(MEM_O + 1, 7, DC)
            residual_group(FFN2, 1, 1.0, ST_FFN2, 4, act_hi, act_lo, "ffn2_norm")
            lows(FFN2, 7, DC)
            gate_up(FFN2, ST_FFN2, 4)
            g = DOWN2 + 1
            lows(g, 0, AHEAD)
            add_residual(DOWN2, 0, 0.5)
            lows(g, AHEAD, 7)
            dve.wait_ge(final_gain_in, 16)
            dve.wait_ge(ssq_ready, 4 * ST_FINAL + 2)
            for t in range(HALVES):
                last = nc.vector.tensor_tensor(h[:, t, 0:COLS], h[:, t, 0:COLS], final_gain[:, 0:COLS],
                                               ALU.mult)
            last.then_inc(tail_gained, 1)
            long_lows(g, 7)
            for t in range(HALVES):
                if t == 0:
                    dve.wait_ge(half_done, 1)
                else:
                    dve.wait_ge(steps_done, BASE[g + 1])
                for s in range(2):
                    cols = h[:, t, COLS + s * SEG:COLS + (s + 1) * SEG]
                    nc.vector.scalar_tensor_tensor(out=cols, in0=banks[:, g % 2, t, s, :], scalar=0.5,
                                                   in1=cols, op0=ALU.mult, op1=ALU.add) \
                        .then_inc(tail_added, 1)
            dve.wait_ge(tail_ssq, 2 * HALVES)
            link(nc.vector.tensor_tensor(ssq[:, ST_FINAL, 1, :], ssq_tail[:, 0, :], ssq_tail[:, 1, :],
                                         ALU.add))
            norm_factor(ST_FINAL, 5, 2)
            dve.wait_ge(rstd_ready, ST_FINAL + 1)
            for t in range(HALVES):
                cols = h[:, t, COLS:D]
                nc.vector.scalar_tensor_tensor(out=cols, in0=cols, scalar=rstd[:, ST_FINAL, t:t + 1],
                                               in1=final_gain[:, COLS:D], op0=ALU.mult,
                                               op1=ALU.mult).then_inc(out_ready_dve, 1)

        @block.tensor
        def _(pe):
            def steps(g, k0, k1, hi, lo, off=0):
                for k in range(k0, k1):
                    n = BASE[g] + k
                    pe.wait_ge(lo_ready, n + 1 + off)
                    first, end = k == 0, k == NSTEPS[g] - 1
                    for t in range(HALVES):
                        tokens = slice(t * P, (t + 1) * P)
                        for a, w in ((hi, w_hi), (hi, w_lo), (lo, w_hi)):
                            for s in range(2):
                                last = nc.tensor.matmul(
                                    banks[:, g % 2, t, s, :], a[:, k, tokens],
                                    w[:, n % RING, s * SEG:(s + 1) * SEG],
                                    start=first and w is w_hi and a is hi,
                                    stop=end and a is lo)
                        if end and g == GROUPS - 1 and t == 0:
                            last.then_inc(half_done, 1)
                    last.then_inc(steps_done, 1)

            def turn_round(g, r, source):
                dst = round_banks(g, r)
                for c in range(4):
                    for t in range(HALVES):
                        last = nc.tensor.transpose(dst[:, c, t * P:(t + 1) * P], source(c, t),
                                                   identity[:, :])
                last.then_inc(turned, 1)

            def of_tok(r):
                return lambda c, t: tok[:, t, (4 * r + c) * P:(4 * r + c + 1) * P]

            def of_rows(src, part):
                return lambda c, t: src[:, t, (4 * part + c) * P:(4 * part + c + 1) * P]

            def turn_group(g, off=0):
                pe.wait_ge(drained, drains_before(g - 1) + 1 + off)
                for r in range(rounds_of(g - 1)):
                    turn_round(g, r, of_tok(r))

            def drains_before(g):
                return sum(1 for at in range(g) if not residual(at))

            def residual(g):
                return DOWN1 <= g < MIX_HB or MIX_OUT <= g < MEM_Q or MEM_O <= g < FFN2 or g >= DOWN2

            def turn_residual(g, number):
                part = (number + 1) % 2
                pe.wait_ge(h_ready, number)
                for r in range(2):
                    turn_round(g, r, of_rows(h, 2 * part + r))

            pe.wait_ge(consts_ready, 2)
            pe.wait_ge(first_in, 16)
            nc.tensor.transpose(banks[:, 1, 0, 0, 0:DC], first_rows, identity[0:DC, 0:DC]) \
                .then_inc(turned, 1)
            pe.wait_ge(pcol_ready, 1)
            pe.wait_ge(x_in[0], 16 * HALVES)
            turn_round(FFN1, 0, of_rows(h, 0))
            pe.wait_ge(x_in[1], 16 * HALVES)
            turn_round(FFN1, 1, of_rows(h, 1))
            pe.wait_ge(taken, 1)
            steps(FFN1, 0, 1, act_hi, act_lo)
            pe.wait_ge(x_in[2], 16 * HALVES)
            turn_round(FFN1, 2, of_rows(h, 2))
            steps(FFN1, 1, 2, act_hi, act_lo)
            pe.wait_ge(taken, 2)
            pe.wait_ge(x_in[3], 16 * HALVES)
            turn_round(FFN1, 3, of_rows(h, 3))
            steps(FFN1, 2, 8, act_hi, act_lo)
            pe.wait_ge(taken, 3)
            steps(FFN1, 8, 12, act_hi, act_lo)
            pe.wait_ge(taken, 4)
            pe.wait_ge(params_in, 16 * PARAM_LOADS)
            for n in range(PTILES):
                last = nc.tensor.transpose(banks[:, 1, 0, 0, n * P:(n + 1) * P], param_rows[:, n, :],
                                           identity[:, :])
            last.then_inc(turned, 1)
            steps(FFN1, 12, DC, act_hi, act_lo)
            pe.wait_ge(pcol_ready, 2)

            def gate_up(first, hi, lo):
                with pe.Fori(0, (GU - 1) // 2) as i:
                    for j in range(2):
                        g = first + 1 + j
                        pe.wait_ge(taken, taken_before(g) + i * 2)
                        steps(g, 0, 4, hi, lo, i * (2 * DC))
                        turn_group(g, i * 2)
                        steps(g, 4, DC, hi, lo, i * (2 * DC))

            gate_up(FFN1, act_hi, act_lo)

            def down(first):
                for j in range(2):
                    g = first + j
                    pe.wait_ge(taken, taken_before(g))
                    steps(g, 0, 4, ffn_hi, ffn_lo)
                    if j == 0:
                        turn_group(g)
                        steps(g, 4, FC - 4, ffn_hi, ffn_lo)
                        pe.wait_ge(taken, taken_before(g) + 1)
                        steps(g, FC - 4, FC, ffn_hi, ffn_lo)
                    elif first == DOWN1:
                        turn_residual(g, 1)
                        steps(g, 4, FC, ffn_hi, ffn_lo)
                    else:
                        steps(g, 4, FC, ffn_hi, ffn_lo)

            down(DOWN1)

            def from_residual(g, number, hi, lo):
                pe.wait_ge(taken, taken_before(g))
                steps(g, 0, 4, hi, lo)
                turn_residual(g, number)
                steps(g, 4, 8, hi, lo)
                pe.wait_ge(taken, taken_before(g) + 2)
                steps(g, 8, DC, hi, lo)

            from_residual(MIX_HB, 2, act_hi, act_lo)
            for g in range(MIX_HB + 1, MEM_K):
                pe.wait_ge(taken, taken_before(g))
                if g >= MIX_HB + 2:
                    pe.wait_ge(copied, g - MIX_HB - 1)
                steps(g, 0, 4, act_hi, act_lo)
                turn_group(g)
                steps(g, 4, 5, act_hi, act_lo)
                if g in MEM_ROUNDS:
                    pe.wait_ge(mem_in, 16 * HALVES)
                    turn_round(g, 1, of_rows(mem_raw, MEM_ROUNDS[g][0]))
                    steps(g, 5, 7, act_hi, act_lo)
                    pe.wait_ge(copied, g - MIX_HB)
                    turn_round(g, 2, of_rows(mem_raw, MEM_ROUNDS[g][1]))
                    steps(g, 7, DC, act_hi, act_lo)
                else:
                    steps(g, 5, DC, act_hi, act_lo)
            for g in range(MEM_K, MIX_OUT):
                pe.wait_ge(taken, taken_before(g))
                if g == MEM_K:
                    pe.wait_ge(copied, 4)
                steps(g, 0, 4, mem_hi, mem_lo)
                if g <= MEM_V:
                    turn_group(g)
                    steps(g, 4, DC, mem_hi, mem_lo)
                else:
                    pe.wait_ge(drained, drains_before(MEM_V) + 1)
                    for r, k0, k1 in ((0, 4, 9), (1, 9, DC)):
                        pe.wait_ge(ln_chunks, r + 1)
                        nc.tensor.matmul(round_banks(g, r)[:, 0, :], ones[:, :], gated[:, 3, :],
                                         start=True, stop=True).then_inc(ln_sum, 1)
                        steps(g, k0, k1, mem_hi, mem_lo)
            g = MIX_OUT
            pe.wait_ge(ln_var, 1)
            pe.wait_ge(y_ready, 1)
            steps(g, 0, 8, act_hi, act_lo)
            pe.wait_ge(y_ready, 2)
            steps(g, 8, DC, act_hi, act_lo)
            g = MIX_OUT + 1
            pe.wait_ge(drained, drains_before(MIX_OUT))
            steps(g, 0, 4, act_hi, act_lo)
            turn_residual(g, 3)
            steps(g, 4, DC, act_hi, act_lo)
            from_residual(MEM_Q, 4, uq_hi, uq_lo)

            def attend_scores(g, pair):
                for head in range(2):
                    for t in range(HALVES):
                        tokens = slice(t * P, (t + 1) * P)
                        n = 0
                        for a, b in ((act_hi, k_hi), (act_hi, k_lo), (act_lo, k_hi)):
                            for c in range(HC):
                                chunk = (2 * pair + head) * HC + c
                                last = nc.tensor.matmul(round_banks(g, 0)[:, 2 * head + t, :],
                                                        a[:, chunk, tokens], b[:, chunk, :],
                                                        start=n == 0, stop=n == 3 * HC - 1)
                                n += 1
                last.then_inc(scores_ready, 1)

            def attend_values(g, pair, head):
                for c in range(HC):
                    cols = slice((head * HC + c) * P, (head * HC + c + 1) * P)
                    n = 0
                    for a, b in ((v_hi, p_hi), (v_lo, p_hi), (v_hi, p_lo)):
                        for m in range(HALVES):
                            last = nc.tensor.matmul(round_banks(g, head)[:, c, :], a[pair][:, m, cols],
                                                    b[:, 2 * head + m, :],
                                                    start=n == 0, stop=n == 3 * HALVES - 1)
                            n += 1
                last.then_inc(turned, 1)

            for g, hi, lo, at in ((MEM_O - 1, uq_hi, uq_lo, (4, 7, 10, 13)),
                                  (MEM_O, k_hi, k_lo, (3, 4, 6, 7))):
                pair = ATTN[g]
                before = taken_before(g)
                pe.wait_ge(taken, before)
                steps(g, 0, at[0], hi, lo)
                turn_group(g)
                steps(g, at[0], at[1], hi, lo)
                pe.wait_ge(taken, before + 2)
                attend_scores(g, pair)
                steps(g, at[1], at[2], hi, lo)
                pe.wait_ge(p_ready, pair + 1)
                turn_round(g, 1, lambda c, t: gated[:, c // 2 * 2 + t, c % 2 * P:(c % 2 + 1) * P])
                steps(g, at[2], at[3], hi, lo)
                pe.wait_ge(taken, before + 3)
                for head in range(2):
                    attend_values(g, pair, head)
                if pair == 0:
                    steps(g, at[3], DC, hi, lo)
                else:
                    steps(g, at[3], 8, hi, lo)
                    pe.wait_ge(taken, before + 5)
                    steps(g, 8, DC, hi, lo)
            g = MEM_O + 1
            pe.wait_ge(taken, taken_before(g))
            steps(g, 0, 4, k_hi, k_lo)
            turn_residual(g, 5)
            steps(g, 4, DC, k_hi, k_lo)
            from_residual(FFN2, 6, act_hi, act_lo)
            gate_up(FFN2, act_hi, act_lo)
            down(DOWN2)


def _param_loads():
    row, loads = 0, 0
    for _, n in PARAMS:
        loads += 1 + (row % P + n - 1) // P
        row += n
    return loads


PARAM_LOADS = _param_loads()

_INS = ["x", "mem", "ffn1_norm", "ffn1_w_gate_up", "ffn1_w_down", "mix_norm", "w_mix_in", "conv_a_w",
        "conv_b_w", "conv_b_bias", "ln_b_gain", "ln_b_bias", "w_mix_out", "mem_q_norm",
        "mem_kv_norm", "w_mem_q", "w_mem_kv", "w_mem_o", "ffn2_norm", "ffn2_w_gate_up",
        "ffn2_w_down", "final_norm"]


def kernel(**inputs):
    import numpy as _np
    import concourse.bacc as _bacc
    from concourse import mybir as _mybir
    from concourse.bass_utils import run_bass_kernel_spmd as _run

    nc = _bacc.Bacc("TRN2", target_bir_lowering=False, num_devices=1, dynamic_dma_scratch_size=512)
    arrays, args = {}, []
    for name in _INS:
        a = _np.ascontiguousarray(inputs[name])
        arrays[f"in_{name}_dram"] = a
        args.append(nc.dram_tensor(f"in_{name}_dram", a.shape, _mybir.dt.from_np(a.dtype),
                                   kind="ExternalInput").ap())
    args.append(nc.dram_tensor("out_dram", (1, TOKENS, D), _mybir.dt.float32,
                               kind="ExternalOutput").ap())
    block_program(nc, *args)
    r = _run(nc, [arrays], core_ids=[0])
    return r.results[0]["out_dram"]
```
